# Optimizing a Trainium2 kernel written in Bass

```python
import jax
import jax.numpy as jnp
from jax import lax
import numpy as np

D_MODEL = 1024
BATCH = 1
SEQ = 256
DEPTH = 2

GRID_W = 64
CTX_LEN = 256

A_HEAD_DIM = 64
A_HEADS = D_MODEL // (2 * A_HEAD_DIM)
A_KV_HEADS = A_HEADS // 4
WINDOW = 128
A_BLOCK = WINDOW
ROPE_BASE = 10000.0
ROPE_AXIS = A_HEAD_DIM // 2

B_DV = 64
B_DK = B_DV // 2
B_HEADS = D_MODEL // (4 * B_DV)
GLA_RANK = 16
GLA_TAU = 16.0
GLA_CHUNK = 16

C_DH = 64
C_HEADS = D_MODEL // (4 * C_DH)
MLSTM_CHUNK = 64
MLSTM_CONV = 3

A_OUT = A_HEADS * A_HEAD_DIM
A_KV = A_KV_HEADS * A_HEAD_DIM
B_KW = B_HEADS * B_DK
B_VW = B_HEADS * B_DV
C_W = C_HEADS * C_DH
MIX_WIDTH = A_OUT + B_VW + C_W
IN_SPLITS = (A_OUT, A_KV, A_KV, B_KW, B_KW, B_VW, B_VW, GLA_RANK, GLA_RANK, C_W, C_W, C_W, 4 * C_HEADS, C_W)
IN_WIDTH = A_OUT + 2 * A_KV + 2 * B_KW + 2 * B_VW + 2 * GLA_RANK + 4 * C_W + 4 * C_HEADS

D_FF = 2816
FFN_RES = 0.5
N_MOD = 9
EPS = 1e-6

kernel_name = 'hybrid_headgroup_diffusion_block'

def rms_norm(x, g):
    xf = x.astype(jnp.float32)
    y = xf * lax.rsqrt(jnp.mean(xf * xf, axis=-1, keepdims=True) + EPS)
    return (y * g.astype(jnp.float32)).astype(x.dtype)

def modulate(x, g, shift, scale):
    return rms_norm(x, g) * (1.0 + scale) + shift

def adaln_params(cvec, w, b):
    m = jax.nn.silu(cvec) @ w + b
    return m.reshape(m.shape[:-1] + (N_MOD, D_MODEL))

def swiglu(u, wg, wu, wd):
    return (jax.nn.silu(u @ wg) * (u @ wu)) @ wd

def ffn_sublayer(x, shift, scale, gate, g_pre, g_post, wg, wu, wd):
    y = swiglu(modulate(x, g_pre, shift, scale), wg, wu, wd)
    return x + FFN_RES * gate * rms_norm(y, g_post)

def split_cols(z):
    parts = []
    start = 0
    for w in IN_SPLITS:
        parts.append(z[..., start:start + w])
        start += w
    return parts

def to_heads(t, n_heads):
    b, t_len, _ = t.shape
    return t.reshape(b, t_len, n_heads, -1).transpose(0, 2, 1, 3)

def from_heads(t):
    b, h, t_len, d = t.shape
    return t.transpose(0, 2, 1, 3).reshape(b, t_len, h * d)

def head_layernorm(o, g):
    of = o.astype(jnp.float32)
    mu = jnp.mean(of, axis=-1, keepdims=True)
    var = jnp.mean(jnp.square(of - mu), axis=-1, keepdims=True)
    y = from_heads((of - mu) * lax.rsqrt(var + EPS))
    return (y * g.astype(jnp.float32)).astype(o.dtype)

def centred_dwconv(x, w):
    k_w = w.shape[0]
    pad = k_w // 2
    t_len = x.shape[1]
    xp = jnp.pad(x, ((0, 0), (pad, pad), (0, 0)))
    out = xp[:, 0:t_len] * w[0]
    for j in range(1, k_w):
        out = out + xp[:, j:j + t_len] * w[j]
    return out

def axial_rope_tables(row_ids, col_ids):
    half = ROPE_AXIS // 2
    inv_freq = ROPE_BASE ** (-jnp.arange(half, dtype=jnp.float32) / half)
    ang_r = row_ids.astype(jnp.float32)[:, None] * inv_freq[None, :]
    ang_c = col_ids.astype(jnp.float32)[:, None] * inv_freq[None, :]
    return (jnp.cos(ang_r)[:, None, :], jnp.sin(ang_r)[:, None, :],
            jnp.cos(ang_c)[:, None, :], jnp.sin(ang_c)[:, None, :])

def axial_rope(x, cos_r, sin_r, cos_c, sin_c):
    def rot(u, cs, sn):
        cs = cs.astype(u.dtype)
        sn = sn.astype(u.dtype)
        hh = u.shape[-1] // 2
        u1, u2 = u[..., :hh], u[..., hh:]
        return jnp.concatenate([u1 * cs - u2 * sn, u1 * sn + u2 * cs], axis=-1)
    return jnp.concatenate([rot(x[..., :ROPE_AXIS], cos_r, sin_r),
                            rot(x[..., ROPE_AXIS:], cos_c, sin_c)], axis=-1)

def windowed_attention(q, k, v, kc, vc, sink):
    b, s_len, hq, d = q.shape
    g = k.shape[2]
    r = hq // g
    nb = s_len // A_BLOCK
    scale = d ** -0.5
    qb = q.reshape(b, nb, A_BLOCK, g, r, d)
    pad = ((0, 0), (A_BLOCK, A_BLOCK), (0, 0), (0, 0))
    kp = jnp.pad(k, pad).reshape(b, nb + 2, A_BLOCK, g, d)
    vp = jnp.pad(v, pad).reshape(b, nb + 2, A_BLOCK, g, d)
    kw = jnp.concatenate([kp[:, :-2], kp[:, 1:-1], kp[:, 2:]], axis=2)
    vw = jnp.concatenate([vp[:, :-2], vp[:, 1:-1], vp[:, 2:]], axis=2)
    qi = jnp.arange(A_BLOCK)[:, None]
    kj = jnp.arange(3 * A_BLOCK)[None, :]
    band = jnp.abs(qi + A_BLOCK - kj) <= WINDOW
    k_abs = (jnp.arange(nb)[:, None] - 1) * A_BLOCK + kj
    mask = band[None] & ((k_abs >= 0) & (k_abs < s_len))[:, None, :]
    s_win = jnp.einsum('bnqgrd,bnkgd->bgrnqk', qb, kw).astype(jnp.float32) * scale
    s_win = jnp.where(mask, s_win, -jnp.inf)
    s_ctx = jnp.einsum('bnqgrd,bcgd->bgrnqc', qb, kc).astype(jnp.float32) * scale
    s_sink = sink.astype(jnp.float32).reshape(1, g, r, 1, 1)
    m = jnp.maximum(jnp.maximum(jnp.max(s_win, axis=-1), jnp.max(s_ctx, axis=-1)), s_sink)
    e_win = jnp.exp(s_win - m[..., None])
    e_ctx = jnp.exp(s_ctx - m[..., None])
    den = jnp.sum(e_win, axis=-1) + jnp.sum(e_ctx, axis=-1) + jnp.exp(s_sink - m)
    o = (jnp.einsum('bgrnqk,bnkgd->bgrnqd', e_win.astype(v.dtype), vw)
         + jnp.einsum('bgrnqc,bcgd->bgrnqd', e_ctx.astype(v.dtype), vc))
    o = o / den[..., None]
    return o.transpose(0, 3, 4, 1, 2, 5).reshape(b, s_len, hq * d).astype(v.dtype)

def context_attention(qc, kc, vc, sink):
    b, l_c, hq, d = qc.shape
    g = kc.shape[2]
    r = hq // g
    s = jnp.einsum('blgrd,bcgd->bgrlc', qc.reshape(b, l_c, g, r, d), kc).astype(jnp.float32) * d ** -0.5
    s_sink = jnp.broadcast_to(sink.astype(jnp.float32).reshape(1, g, r, 1, 1), s.shape[:-1] + (1,))
    p = jax.nn.softmax(jnp.concatenate([s, s_sink], axis=-1), axis=-1)[..., :l_c]
    o = jnp.einsum('bgrlc,bcgd->blgrd', p.astype(vc.dtype), vc)
    return o.reshape(b, l_c, hq * d)

def gla_chunked(q, k, v, log_a, state):
    b, h, t_len, dk = q.shape
    dv = v.shape[-1]
    lc = GLA_CHUNK
    n = t_len // lc
    qf = q.astype(jnp.float32).reshape(b, h, n, lc, dk)
    kf = k.astype(jnp.float32).reshape(b, h, n, lc, dk)
    vf = v.astype(jnp.float32).reshape(b, h, n, lc, dv)
    bcum = jnp.cumsum(log_a.astype(jnp.float32).reshape(b, h, n, lc, dk), axis=3)
    b_last = bcum[:, :, :, -1]
    causal = jnp.tril(jnp.ones((lc, lc), dtype=bool))[:, :, None]
    decay = jnp.exp(jnp.where(causal, bcum[:, :, :, :, None, :] - bcum[:, :, :, None, :, :], -jnp.inf))
    attn = jnp.einsum('bhntd,bhnsd,bhntsd->bhnts', qf, kf, decay)
    o_intra = jnp.einsum('bhnts,bhnsv->bhntv', attn, vf)
    s_loc = jnp.einsum('bhnsd,bhnsv->bhndv', kf * jnp.exp(b_last[:, :, :, None, :] - bcum), vf)

    def step(s, inp):
        bl, sl = inp
        return jnp.exp(bl)[..., None] * s + sl, s

    s_final, s_prev = lax.scan(step, state, (jnp.moveaxis(b_last, 2, 0), jnp.moveaxis(s_loc, 2, 0)))
    s_prev = jnp.moveaxis(s_prev, 0, 2)
    o = o_intra + jnp.einsum('bhntd,bhndv->bhntv', qf * jnp.exp(bcum), s_prev)
    return o.reshape(b, h, t_len, dv).astype(v.dtype), s_final

def mlstm_chunked(q, k, v, log_i, log_f, state):
    b, h, t_len, d = q.shape
    lc = MLSTM_CHUNK
    n_ch = t_len // lc
    qf = q.astype(jnp.float32).reshape(b, h, n_ch, lc, d)
    kf = k.astype(jnp.float32).reshape(b, h, n_ch, lc, d)
    vf = v.astype(jnp.float32).reshape(b, h, n_ch, lc, d)
    li = log_i.astype(jnp.float32).reshape(b, h, n_ch, lc)
    bcum = jnp.cumsum(log_f.astype(jnp.float32).reshape(b, h, n_ch, lc), axis=-1)
    b_last = bcum[..., -1]
    causal = jnp.tril(jnp.ones((lc, lc), dtype=bool))
    dmat = jnp.where(causal, bcum[..., :, None] - bcum[..., None, :] + li[..., None, :], -jnp.inf)
    g_end = b_last[..., None] - bcum + li
    m_loc = jnp.max(g_end, axis=-1)
    w_end = jnp.exp(g_end - m_loc[..., None])
    c_loc = jnp.einsum('bhns,bhnsv,bhnsk->bhnvk', w_end, vf, kf)
    n_loc = jnp.einsum('bhns,bhnsk->bhnk', w_end, kf)

    def step(carry, inp):
        c_st, n_st, m_st = carry
        bl, ml, cl, nl = inp
        m_new = jnp.maximum(bl + m_st, ml)
        a = jnp.exp(bl + m_st - m_new)
        e = jnp.exp(ml - m_new)
        c_new = a[..., None, None] * c_st + e[..., None, None] * cl
        n_new = a[..., None] * n_st + e[..., None] * nl
        return (c_new, n_new, m_new), (c_st, n_st, m_st)

    xs = (jnp.moveaxis(b_last, 2, 0), jnp.moveaxis(m_loc, 2, 0), jnp.moveaxis(c_loc, 2, 0), jnp.moveaxis(n_loc, 2, 0))
    final, (c_prev, n_prev, m_prev) = lax.scan(step, state, xs)
    c_prev = jnp.moveaxis(c_prev, 0, 2)
    n_prev = jnp.moveaxis(n_prev, 0, 2)
    m_prev = jnp.moveaxis(m_prev, 0, 2)
    inter = bcum + m_prev[..., None]
    m_t = jnp.maximum(inter, jnp.max(dmat, axis=-1))
    a_t = jnp.exp(inter - m_t)
    sc = jnp.einsum('bhntd,bhnsd->bhnts', qf, kf) * jnp.exp(dmat - m_t[..., None])
    num = a_t[..., None] * jnp.einsum('bhntk,bhnvk->bhntv', qf, c_prev) + jnp.einsum('bhnts,bhnsv->bhntv', sc, vf)
    den = a_t * jnp.einsum('bhntk,bhnk->bhnt', qf, n_prev) + jnp.sum(sc, axis=-1)
    hid = num / jnp.maximum(jnp.abs(den), jnp.exp(-m_t))[..., None]
    return hid.reshape(b, h, t_len, d).astype(v.dtype), final

def bidirectional(scan_fn, state0, lat, ctx, need_ctx):
    def flip(ts):
        return tuple(jnp.flip(t, axis=2) for t in ts)
    (cqkv, cgf, cgb), (lqkv, lgf, lgb) = ctx, lat
    oc_f, sc_f = scan_fn(*cqkv, *cgf, state0)
    oc_b, sc_b = scan_fn(*flip(cqkv), *flip(cgb), state0)
    o_f, _ = scan_fn(*lqkv, *lgf, sc_f)
    o_b, _ = scan_fn(*flip(lqkv), *flip(lgb), sc_b)
    o = o_f + jnp.flip(o_b, axis=2)
    oc = oc_f + jnp.flip(oc_b, axis=2) if need_ctx else None
    return o, oc

def token_mixing(u, uc, rope, w_in, b_in, w_out, sink, gla_wa, gla_ba, gla_g, conv_w, f_bias, mlstm_g, need_ctx):
    b, t_len, _ = u.shape
    l_c = uc.shape[1]
    pl = split_cols(u @ w_in + b_in)
    pc = split_cols(uc @ w_in + b_in)

    q = axial_rope(pl[0].reshape(b, t_len, A_HEADS, A_HEAD_DIM), *rope)
    k = axial_rope(pl[1].reshape(b, t_len, A_KV_HEADS, A_HEAD_DIM), *rope)
    v = pl[2].reshape(b, t_len, A_KV_HEADS, A_HEAD_DIM)
    kc = pc[1].reshape(b, l_c, A_KV_HEADS, A_HEAD_DIM)
    vc = pc[2].reshape(b, l_c, A_KV_HEADS, A_HEAD_DIM)
    y_a = windowed_attention(q, k, v, kc, vc, sink)

    def gla_inputs(p):
        qkv = (to_heads(p[3], B_HEADS) * B_DK ** -0.5, to_heads(p[4], B_HEADS), to_heads(p[5], B_HEADS))
        def gate(dirn):
            z = (p[7 + dirn] @ gla_wa[dirn] + gla_ba[dirn]).astype(jnp.float32)
            return (to_heads(jax.nn.log_sigmoid(z) / GLA_TAU, B_HEADS),)
        return qkv, gate(0), gate(1)
    gla_state0 = jnp.zeros((b, B_HEADS, B_DK, B_DV), jnp.float32)
    o_b, oc_b = bidirectional(gla_chunked, gla_state0, gla_inputs(pl), gla_inputs(pc), need_ctx)
    y_b = jax.nn.silu(pl[6]) * head_layernorm(o_b, gla_g)

    def mlstm_inputs(p):
        qk = jax.nn.silu(centred_dwconv(jnp.concatenate([p[9], p[10]], axis=-1), conv_w))
        qkv = (to_heads(qk[..., :C_W], C_HEADS), to_heads(qk[..., C_W:], C_HEADS) * C_DH ** -0.5, to_heads(p[11], C_HEADS))
        gt = p[12].astype(jnp.float32).reshape(p[12].shape[:2] + (4, C_HEADS)).transpose(2, 0, 3, 1)
        fwd = (gt[0], jax.nn.log_sigmoid(gt[1] + f_bias[0][None, :, None]))
        bwd = (gt[2], jax.nn.log_sigmoid(gt[3] + f_bias[1][None, :, None]))
        return qkv, fwd, bwd
    mstate0 = (jnp.zeros((b, C_HEADS, C_DH, C_DH), jnp.float32),
               jnp.zeros((b, C_HEADS, C_DH), jnp.float32),
               jnp.zeros((b, C_HEADS), jnp.float32))
    o_c, oc_c = bidirectional(mlstm_chunked, mstate0, mlstm_inputs(pl), mlstm_inputs(pc), need_ctx)
    y_c = jax.nn.sigmoid(pl[13]) * head_layernorm(o_c, mlstm_g)

    y = jnp.concatenate([y_a, y_b, y_c], axis=-1) @ w_out
    if not need_ctx:
        return y, None
    qc = pc[0].reshape(b, l_c, A_HEADS, A_HEAD_DIM)
    yc_a = context_attention(qc, kc, vc, sink)
    yc_b = jax.nn.silu(pc[6]) * head_layernorm(oc_b, gla_g)
    yc_c = jax.nn.sigmoid(pc[13]) * head_layernorm(oc_c, mlstm_g)
    yc = jnp.concatenate([yc_a, yc_b, yc_c], axis=-1) @ w_out
    return y, yc

def setup_inputs(seed: int = 0) -> dict:
    key = jax.random.key(seed)
    ks = jax.random.split(key, 24)

    def nrm(k, shape, s):
        return jax.random.normal(k, shape, jnp.float32) * s

    n_l = DEPTH
    return {
        'x': nrm(ks[0], (BATCH, SEQ, D_MODEL), 1.0),
        'c': nrm(ks[1], (BATCH, D_MODEL), 1.0),
        'ctx': nrm(ks[2], (BATCH, CTX_LEN, D_MODEL), 1.0),
        'c_ctx': nrm(ks[3], (D_MODEL,), 1.0),
        'ada_w': nrm(ks[4], (n_l, D_MODEL, N_MOD * D_MODEL), D_MODEL ** -0.5),
        'ada_b': nrm(ks[5], (n_l, N_MOD * D_MODEL), 0.02),
        'norm_g': 1.0 + nrm(ks[6], (n_l, 6, D_MODEL), 0.02),
        'ffn1_wg': nrm(ks[7], (n_l, D_MODEL, D_FF), D_MODEL ** -0.5),
        'ffn1_wu': nrm(ks[8], (n_l, D_MODEL, D_FF), D_MODEL ** -0.5),
        'ffn1_wd': nrm(ks[9], (n_l, D_FF, D_MODEL), D_FF ** -0.5),
        'ffn2_wg': nrm(ks[10], (n_l, D_MODEL, D_FF), D_MODEL ** -0.5),
        'ffn2_wu': nrm(ks[11], (n_l, D_MODEL, D_FF), D_MODEL ** -0.5),
        'ffn2_wd': nrm(ks[12], (n_l, D_FF, D_MODEL), D_FF ** -0.5),
        'w_in': nrm(ks[13], (n_l, D_MODEL, IN_WIDTH), D_MODEL ** -0.5),
        'b_in': nrm(ks[14], (n_l, IN_WIDTH), 0.02),
        'w_out': nrm(ks[15], (n_l, MIX_WIDTH, D_MODEL), MIX_WIDTH ** -0.5),
        'attn_sink': nrm(ks[16], (n_l, A_HEADS), 0.5),
        'gla_w_alpha': nrm(ks[17], (n_l, 2, GLA_RANK, B_KW), GLA_RANK ** -0.5),
        'gla_b_alpha': nrm(ks[18], (n_l, 2, B_KW), 0.1),
        'gla_norm': 1.0 + nrm(ks[19], (n_l, B_VW), 0.02),
        'mlstm_conv': nrm(ks[20], (n_l, MLSTM_CONV, 2 * C_W), MLSTM_CONV ** -0.5),
        'mlstm_f_bias': jnp.linspace(3.0, 6.0, C_HEADS, dtype=jnp.float32) + nrm(ks[21], (n_l, 2, C_HEADS), 0.1),
        'mlstm_norm': 1.0 + nrm(ks[22], (n_l, C_W), 0.02),
    }

def reference(x, c, ctx, c_ctx, ada_w, ada_b, norm_g, ffn1_wg, ffn1_wu, ffn1_wd, ffn2_wg, ffn2_wu, ffn2_wd,
              w_in, b_in, w_out, attn_sink, gla_w_alpha, gla_b_alpha, gla_norm, mlstm_conv, mlstm_f_bias, mlstm_norm):
    s_len = x.shape[1]
    rows = s_len // GRID_W
    row_ids = jnp.broadcast_to(jnp.arange(rows)[:, None], (rows, GRID_W)).reshape(-1)
    col_ids = jnp.broadcast_to(jnp.arange(GRID_W)[None, :], (rows, GRID_W)).reshape(-1)
    rope = axial_rope_tables(row_ids, col_ids)

    h, hc = x, ctx
    for layer in range(DEPTH):
        need_ctx = layer < DEPTH - 1
        mod = adaln_params(c, ada_w[layer], ada_b[layer])[:, :, None, :]
        modc = adaln_params(c_ctx, ada_w[layer], ada_b[layer])
        g = norm_g[layer]

        h = ffn_sublayer(h, mod[:, 0], mod[:, 1], mod[:, 2], g[0], g[1], ffn1_wg[layer], ffn1_wu[layer], ffn1_wd[layer])
        hc = ffn_sublayer(hc, modc[0], modc[1], modc[2], g[0], g[1], ffn1_wg[layer], ffn1_wu[layer], ffn1_wd[layer])

        y, yc = token_mixing(modulate(h, g[2], mod[:, 3], mod[:, 4]), modulate(hc, g[2], modc[3], modc[4]), rope,
                             w_in[layer], b_in[layer], w_out[layer], attn_sink[layer],
                             gla_w_alpha[layer], gla_b_alpha[layer], gla_norm[layer],
                             mlstm_conv[layer], mlstm_f_bias[layer], mlstm_norm[layer], need_ctx)
        h = h + mod[:, 5] * rms_norm(y, g[3])

        h = ffn_sublayer(h, mod[:, 6], mod[:, 7], mod[:, 8], g[4], g[5], ffn2_wg[layer], ffn2_wu[layer], ffn2_wd[layer])
        if need_ctx:
            hc = hc + modc[5] * rms_norm(yc, g[3])
            hc = ffn_sublayer(hc, modc[6], modc[7], modc[8], g[4], g[5], ffn2_wg[layer], ffn2_wu[layer], ffn2_wd[layer])
    return h


_drawn_inputs = setup_inputs


def setup_inputs(seed=0):
    import zlib

    import numpy as np

    out = dict(_drawn_inputs(seed))
    spreads = {}
    factors = {}
    for name, (base, spread) in spreads.items():
        noise = np.random.default_rng([zlib.crc32(name.encode()), seed]).standard_normal(out[name].shape)
        drawn = base * np.exp(spread * noise) if base else spread * noise
        out[name] = jnp.asarray(drawn.astype(out[name].dtype))
    for name, factor in factors.items():
        out[name] = (out[name] * factor).astype(out[name].dtype)
    return out
```

```python
import math
from contextlib import ExitStack

import concourse.bass as bass
from concourse import mybir

ALU = mybir.AluOpType
ACT = mybir.ActivationFunctionType
F32 = mybir.dt.float32
F32R = mybir.dt.float32r
U32 = mybir.dt.uint32
AX_X = mybir.AxisListType.X

P = 128
DM = 1024
KT = DM // P
LAT = 256
CTX = 256
TOK = LAT + CTX
TT = TOK // P
DEPTH = 2
D_FF = 2816
FT = D_FF // P
N_MOD = 9
MOD_TILES = N_MOD * KT
FIRST_GROUPS = 5
FIRST_TILES = 4 * FIRST_GROUPS
EPS = 1e-6

A_HEADS, A_DIM, A_GROUPS = 8, 64, 2
B_HEADS, B_DK, B_DV = 4, 32, 64
C_HEADS, C_DIM = 4, 64
RANK, TAU = 16, 16.0
FFN_RES = 0.5
NEG = -1e30

COL_Q, COL_K, COL_V = 0, 512, 640
COL_GQ, COL_GK, COL_GV, COL_GG = 768, 896, 1024, 1280
COL_RANK = 1536
COL_MQ, COL_MK, COL_MV = 1568, 1824, 2080
COL_GATE, COL_OG = 2336, 2352

TILE_COLS = ([COL_Q + P * j for j in range(4)] + [COL_GQ, COL_GG, COL_GG + P, COL_OG, COL_OG + P]
             + [COL_MQ, COL_MQ + P, COL_MK, COL_MK + P, COL_MV, COL_MV + P, COL_K, COL_V, COL_GK, COL_GV, COL_GV + P])
T_Q, T_GQ, T_GG, T_OG, T_MQ, T_MV, T_K, T_V, T_GK, T_GV, T_SMALL = 0, 4, 5, 7, 9, 13, 15, 16, 17, 18, 20
LAT_ONLY = 10
N_PROJ = 21
V_TILES = [T_V, T_GV, T_GV + 1]
GATE_ROW = 32

V_ADA, V_NORM = 0, MOD_TILES
V_BIN, V_CONV = 0, N_PROJ
V_GLAN = V_CONV + 12
V_MLN = V_GLAN + 2
V_BA = V_MLN + 2
N_VEC2 = V_BA + 2

LEVELS = [128, 64, 32, 16, 8, 4, 2, 1]
MASKED = LEVELS[2:]


BIAS_RUNS = []
for _j, _col in enumerate(TILE_COLS):
    if BIAS_RUNS and BIAS_RUNS[-1][1] + P * BIAS_RUNS[-1][2] == _col:
        BIAS_RUNS[-1][2] += 1
    else:
        BIAS_RUNS.append([_j, _col, 1])


def weight_units():
    units = []
    for layer in range(DEPTH):
        for q in range(2):
            units += [(f"gu{q}", layer, 2 * KT * P)] * FT
            units += [(f"dn{q}", layer, FT // 2 * P)] * (2 * KT)
            if q == 0:
                units += [("in", layer, 2 * KT * P)] * (N_PROJ // 2)
                units += [("small", layer, KT * P)]
                units += [("out", layer, 2 * KT * P)] * (KT // 2)
    return units


def hybrid_block_kernel(nc, x, c, ctx_in, c_ctx, ada_w, ada_b, norm_g, ffn1_wg, ffn1_wu, ffn1_wd, ffn2_wg, ffn2_wu,
                        ffn2_wd, w_in, b_in, w_out, attn_sink, gla_w_alpha, gla_b_alpha, gla_norm, mlstm_conv,
                        mlstm_f_bias, mlstm_norm, k_ident, k_rot, k_swap, k_cos, k_sin, k_band, k_level, k_sel, out):
    units = weight_units()
    with ExitStack() as stack:
        cursor = [(nc.sbuf_base + 63) // 64 * 64]

        def sized(shape, dt):
            return (math.prod(shape[1:]) * 4 + 31) // 32 * 32

        def place(name, shape, dt, offset):
            return nc.alloc_sbuf_tensor_at(name, shape, dt, offset=offset)

        def own(name, shape, dt=F32):
            offset = cursor[0]
            cursor[0] += sized(shape, dt)
            return place(name, shape, dt, offset)

        def overlay(start, size, tensors):
            made, offset = [], start
            for name, shape, dt in tensors:
                made.append(place(name, shape, dt, offset))
                offset += sized(shape, dt)
            assert offset <= start + size, (tensors[0][0], offset - start, size)
            return made

        ROWB = KT * TOK * 4
        H = own("H", [P, KT, TOK])
        U_AT, U_SIZE = cursor[0], 2 * ROWB
        cursor[0] += U_SIZE
        HT_AT, HT_SIZE = cursor[0], 2 * FT * TOK * 4
        cursor[0] += HT_SIZE
        raw = [own(f"raw{s}", [P, 2 * KT * P]) for s in range(2)]
        w_hi = [own(f"w_hi{s}", [P, 2 * KT * P], F32R) for s in range(2)]
        w_lo = [own(f"w_lo{s}", [P, 2 * KT * P], F32R) for s in range(2)]
        ADA_AT = cursor[0]
        ada_slot = [own(f"ada_slot{s}", [P, KT, P]) for s in range(2)]
        tmp_a = [own(f"tmp_a{i}", [P, TOK]) for i in range(2)]
        tmp_b = [own(f"tmp_b{i}", [P, TOK]) for i in range(2)]
        sq_sum = tmp_b[0]
        rstd = own("rstd", [P, TOK])
        ident = own("ident", [P, P])
        ones = own("ones", [P, P])
        mod = [own(f"mod{la}", [P, N_MOD, KT, 2]) for la in range(DEPTH)]
        vec1 = [own(f"vec1_{la}", [P, MOD_TILES + 6 * KT]) for la in range(DEPTH)]
        vec2 = [own(f"vec2_{la}", [P, N_VEC2]) for la in range(DEPTH)]
        silu_c = own("silu_c", [P, 2 * KT])
        eps_col = own("eps_col", [P, 1])
        assert cursor[0] <= nc.sbuf_top, (cursor[0], nc.sbuf_top)

        u_hi, u_lo = overlay(U_AT, U_SIZE, [("u_hi", [P, KT, TOK], F32R), ("u_lo", [P, KT, TOK], F32R)])
        ht_hi, ht_lo = overlay(HT_AT, HT_SIZE, [("ht_hi", [P, FT, TOK], F32R), ("ht_lo", [P, FT, TOK], F32R)])
        (Y_ffn,) = overlay(U_AT, U_SIZE, [("Y_ffn", [P, KT, TOK], F32)])
        (Y_mix,) = overlay(HT_AT, HT_SIZE, [("Y_mix", [P, KT, TOK], F32)])

        (first_u,) = overlay(U_AT, U_SIZE, [("ada_first_u", [P, KT, 4 * P], F32)])
        (rows_x, rows_c, *rest) = overlay(HT_AT, HT_SIZE, [
            ("rows_x", [P, TT, DM], F32), ("rows_c", [2 * KT, P], F32),
            *((f"rows_v{i}", [P, P], F32) for i in range(2 * DEPTH)),
            *((f"ada_first{g}", [P, KT, 4 * P], F32) for g in range(FIRST_GROUPS - 1))])
        rows_v, ada_first = rest[:2 * DEPTH], rest[2 * DEPTH:] + [first_u]

        (proj, v_tok, vm_tok, y_tok, rot, swap, cos, sin, band, level_mask, w_alpha, sink, gate_sel, f_bias,
         gla_cross) = overlay(HT_AT, HT_SIZE, [
             ("proj", [P, N_PROJ, TOK], F32), ("v_tok", [P, TT, 3 * P], F32),
             ("vm_tok", [P, TT, C_HEADS, C_DIM + 1], F32), ("y_tok", [P, TT, DM], F32), ("rot", [P, P], F32),
             ("swap", [P, P], F32), ("cos", [P, LAT], F32), ("sin", [P, LAT], F32), ("band", [P, 2, P], F32),
             ("level_mask", [P, len(MASKED) + 1, P], F32), ("w_alpha", [2 * RANK, 2, P], F32),
             ("sink", [P, A_HEADS], F32), ("gate_sel", [GATE_ROW + 4 * C_HEADS, 2, 64], F32),
             ("f_bias", [64, 1], F32), ("gla_cross", [P, B_HEADS, 2, LAT], F32)])
        (gla_pair,) = overlay(HT_AT, HT_SIZE, [("gla_pair", [P, B_HEADS, TT, P], F32)])
        hid, hid_tmp = overlay(HT_AT, HT_SIZE, [("hid", [P, TT, C_HEADS, C_DIM], F32), ("hid_tmp", [P, TT, C_DIM], F32)])
        (qk_conv,) = overlay(ADA_AT, ROWB // 2, [("qk_conv", [P, 4, TOK], F32)])

        n_att = A_HEADS * TT
        (rope_tmp,) = overlay(U_AT, U_SIZE, [("rope_tmp", [P, 5, LAT], F32)])
        (k_swapped, prob0, prob1, prob2, pt0, pt1, row_max, neg_max, row_sum, sink_exp, neg_sink) = overlay(
            U_AT, U_SIZE, [("k_swapped", [P, TOK], F32), *((f"probs{i}", [P, TOK], F32) for i in range(3)),
                           *((f"probs_t{i}", [P, 4, P], F32) for i in range(2)),
                           *((n, [P, n_att], F32) for n in ("row_max", "neg_max", "row_sum", "sink_exp")),
                           ("neg_sink", [P, A_HEADS], F32)])
        probs, probs_t = [prob0, prob1, prob2], [pt0, pt1]
        (gla_cum, gx0, gx1, gk0, gk1, gla_diag, bt_col) = overlay(U_AT, U_SIZE, [
            *((n, [P, 2, TOK], F32) for n in ("gla_cum", "gla_x0", "gla_x1", "gla_kq0", "gla_kq1")),
            ("gla_diag", [P, B_HEADS, TT, P], F32), ("bt_col", [P, 2], F32)])
        gla_x, gla_kq = [gx0, gx1], [gk0, gk1]
        gla_z = gk0
        (g_f, g_i, g_b, g_max, wc0, wc1, xg0, xg1, a_col, em_col, c_den) = overlay(U_AT, U_SIZE, [
            *((n, [64, TOK], F32) for n in ("g_f", "g_i", "g_b", "g_max")),
            *((f"w_c{i}", [P, 3, 2, LAT], F32) for i in range(2)), *((f"xg{i}", [P, TT, P], F32) for i in range(2)),
            *((n, [P, TT, 64], F32) for n in ("a_col", "em_col")), ("c_den", [P, TT], F32)])
        w_c, xg = [wc0, wc1], [xg0, xg1]
        ln_c, ln_sq, ln_s = overlay(U_AT, U_SIZE, [
            ("ln_c", [P, TT * 4, 64], F32), ("ln_sq", [P, TT * 4, 64], F32), ("ln_s", [P, 4, TT * 4], F32)])

        bank = [stack.enter_context(nc.psum_tensor(f"bank{i}", [P, 512], F32)) for i in range(8)]
        mod_acc = bank[6][:, 0:2 * MOD_TILES]

        def sem(name):
            return stack.enter_context(nc.semaphore(name))

        raw_loaded = [sem(f"raw_loaded{s}") for s in range(2)]
        hi_ready = [sem(f"hi_ready{s}") for s in range(2)]
        lo_ready = [sem(f"lo_ready{s}") for s in range(2)]
        unit_used = [sem(f"unit_used{s}") for s in range(2)]
        ada_loaded = [sem(f"ada_loaded{s}") for s in range(2)]
        ada_used = [sem(f"ada_used{s}") for s in range(2)]
        first_loaded = [sem(f"first_loaded{g}") for g in range(FIRST_GROUPS)]
        first_used = sem("first_used")
        (c_loaded, x_loaded, ones_ready, eps_ready, rows_cleared, rows_loaded, c_silu, c_turned, c_ready, x_turned, x_copied,
         rows_turned, vec_ready, mod_step, out_turned, out_copied, out_stored, mix_cleared, mix_loaded) = (
            sem(n) for n in ("c_loaded", "x_loaded", "ones_ready", "eps_ready", "rows_cleared", "rows_loaded", "c_silu",
                             "c_turned", "c_ready", "x_turned", "x_copied", "rows_turned", "vec_ready", "mod_step",
                             "out_turned", "out_copied", "out_stored", "mix_cleared", "mix_loaded"))
        NORM = ("sq_ready", "sq_used", "rms_ready", "rstd_ready", "scaled", "moded", "uhi_ready", "u_ready")
        GATED = ("silu_ready", "prod_ready", "hthi_ready", "ht_ready")
        POST = ("y_ready", "ysq_ready", "ysq_added", "ss_done", "ss_rms", "ss_rstd", "y_scaled", "h_added")
        MIX = ("proj_ready", "v_turned", "v_ready", "vm_ready", "rot_done", "rope_step", "swap_done",
               "swap_ready", "score", "max_step", "exp_done", "turned", "pt_ready", "pv_done", "o_ready", "sink_step",
               "sink_done", "gla_z_mm", "gla_z_ready", "gla_act", "gla_la", "gla_cum_ready", "gla_bt", "gla_q",
               "gla_xk", "gla_xq", "gla_ex", "gla_k", "gla_qs", "gla_mm", "gla_put_act", "gla_put", "gla_cx",
               "gla_cqk", "gla_cmm", "gla_cput", "gla_o", "gla_ln", "gla_sqrt", "conv", "qk_ready", "gate_mm",
               "gate_row", "gate_act", "gate_turned", "gate_col", "kq_done", "g_done", "xg_ready", "w_ready",
               "p_ready", "num_done", "hid_step", "ml_ln", "ml_sqrt", "y_tok_ready", "yt_turned", "yt_full", "yt_hi", "yt_ready")
        norm = {n: sem(n) for n in NORM}
        gated = {n: sem(n) for n in GATED}
        post = {n: sem(n) for n in POST}
        mixer = {n: sem(n) for n in MIX}

        def wait(eng, semaphore, value):
            if not (isinstance(value, int) and value <= 0):
                eng.wait_ge(semaphore, value)

        def steps(eng, count, body):
            body(0)
            with eng.Fori(1, count - 1) as i:
                body(i)
            body(count - 1)

        def split_hi(act, n, i=0, per=1):
            if n >= len(units):
                return
            s, k, size = n % 2, n // 2 + per * i, units[n][2]
            act.wait_ge(raw_loaded[s], 32 * k + 32)
            wait(act, unit_used[s], k)
            nc.scalar.activation(w_hi[s][:, 0:size], raw[s][:, 0:size], ACT.Copy).then_inc(hi_ready[s], 1)

        def split_lo(dve, n, i=0, per=1):
            if n >= len(units):
                return
            s, k, size = n % 2, n // 2 + per * i, units[n][2]
            dve.wait_ge(hi_ready[s], k + 1)
            nc.vector.tensor_tensor(w_lo[s][:, 0:size], raw[s][:, 0:size], w_hi[s][:, 0:size].bitcast(F32),
                                    ALU.subtract).then_inc(lo_ready[s], 1)

        def ahead_of(split, eng, n0, i, per, ahead):
            if isinstance(i, int):
                split(eng, n0 + per * i + ahead)
            else:
                split(eng, n0 + ahead, i, per // 2)

        def unit_done(eng, n0, i, per, j):
            eng.wait_ge(unit_used[(n0 + j) % 2], (n0 + j) // 2 + i * (per // 2) + 1)

        def products(acc, wh, wl, xh, xl, first, last):
            nc.tensor.matmul(acc, wh, xh, start=first, stop=False)
            nc.tensor.matmul(acc, wh, xl, start=False, stop=False)
            return nc.tensor.matmul(acc, wl, xh, start=False, stop=last)

        def tile_of(buf, at, k):
            return buf[:, at + k * P:at + (k + 1) * P]

        ada_parts = {}
        place_in_order = 0
        for name, la, j0, count in ((("beside", 0, 0), 0, FIRST_TILES, 2 * FT), ("down", 0, FIRST_TILES + 2 * FT, KT),
                                    (("turn", 0), 1, 0, KT), (("turn", 1), 1, KT, KT), (("beside", 0, 1), 1, 2 * KT, FT),
                                    (("apart", 1), 1, 2 * KT + FT, 12), (("beside", 1, 0), 1, 2 * KT + FT + 12, FT)):
            ada_parts[name] = (la, j0, count, place_in_order)
            place_in_order += count

        def ada_done(name):
            return ada_parts[name][2] + ada_parts[name][3]

        assert place_in_order == DEPTH * MOD_TILES - FIRST_TILES

        ffn_w = {0: (ffn1_wg, ffn1_wu, ffn1_wd), 1: (ffn2_wg, ffn2_wu, ffn2_wd)}
        first_unit = {}
        for n, (kind, layer, _) in enumerate(units):
            first_unit.setdefault((kind, layer), n)

        def width(layer, part):
            return LAT if layer == DEPTH - 1 and part > 0 else TOK

        block = stack.enter_context(nc.Block())

        @block.sync
        def _(sp):
            sp.dma_start(rows_c[0:KT, :], c.rearrange("a (k p) -> (a k) p", p=P)).then_inc(c_loaded, 16)
            sp.dma_start(rows_c[KT:2 * KT, :], c_ctx.rearrange("(k p) -> k p", p=P)).then_inc(c_loaded, 16)
            sp.dma_start(ident[:], k_ident).then_inc(c_loaded, 16)
            sp.dma_start(rows_x[:, 0:2, :], x.rearrange("a (t p) d -> p (a t) d", p=P)).then_inc(x_loaded, 16)
            sp.dma_start(rows_x[:, 2:4, :], ctx_in.rearrange("a (t p) d -> p (a t) d", p=P)).then_inc(x_loaded, 16)

            for g in range(FIRST_GROUPS):
                sp.dma_start(ada_first[g][:], ada_w[0].rearrange("(k p) f -> p k f", p=P)[:, :, g * 4 * P:(g + 1) * 4 * P])\
                    .then_inc(first_loaded[g], 16)

            def gate_up(layer, q):
                n0 = first_unit[f"gu{q}", layer]
                src = [w[layer].rearrange("(k p) f -> p k f", p=P) for w in ffn_w[q][0:2]]

                def body(i):
                    for j in range(2):
                        s, k = (n0 + j) % 2, (n0 + j) // 2 + i
                        wait(sp, lo_ready[s], k)
                        for w in range(2):
                            sp.dma_start(raw[s][:, w * DM:(w + 1) * DM].rearrange("p (k c) -> p k c", k=KT),
                                         src[w][:, :, bass.ds(i * (2 * P) + j * P, P)]).then_inc(raw_loaded[s], 16)
                steps(sp, FT // 2, body)

            def down(layer, q):
                n0 = first_unit[f"dn{q}", layer]
                src = ffn_w[q][2][layer].rearrange("(k p) d -> p k d", p=P)
                half = FT // 2

                def body(i):
                    for j in range(2):
                        s, k = (n0 + j) % 2, (n0 + j) // 2 + i
                        wait(sp, lo_ready[s], k)
                        dst = raw[s][:, 0:half * P].rearrange("p (k c) -> p k c", k=half)
                        for k0, k1 in ((0, 6), (6, half)):
                            sp.dma_start(dst[:, k0:k1, :], src[:, j * half + k0:j * half + k1, bass.ds(i * P, P)])\
                                .then_inc(raw_loaded[s], 16)
                steps(sp, KT, body)

            def tiles(n, src, runs):
                s = n % 2
                sp.wait_ge(lo_ready[s], n // 2)
                for at, col, m in runs:
                    dst = raw[s][:, at // P * P * KT:(at // P + 1) * P * KT].rearrange("p (k c) -> p k c", k=KT)
                    sp.dma_start(dst[:, :, at % P:at % P + m], src[:, :, col:col + m]).then_inc(raw_loaded[s], 16)

            for layer in range(DEPTH):
                gate_up(layer, 0)
                down(layer, 0)
                src = w_in[layer].rearrange("(k p) f -> p k f", p=P)
                for u in range(N_PROJ // 2):
                    tiles(first_unit["in", layer] + u, src, [(0, TILE_COLS[2 * u], P), (P, TILE_COLS[2 * u + 1], P)])
                tiles(first_unit["small", layer], src, [(0, COL_RANK, 2 * RANK), (GATE_ROW, COL_GATE, 4 * C_HEADS)])
                src = w_out[layer].rearrange("(k p) f -> p k f", p=P)
                for u in range(KT // 2):
                    tiles(first_unit["out", layer] + u, src, [(0, 2 * u * P, P), (P, (2 * u + 1) * P, P)])
                gate_up(layer, 1)
                down(layer, 1)
            for t in range(LAT // P):
                sp.wait_ge(out_copied, 2 * t + 2)
                sp.dma_start(out[0, t * P:(t + 1) * P, :], Y_ffn[:, 2 * t:2 * t + 2, :].rearrange("p a b -> p (a b)"))\
                    .then_inc(out_stored, 16)
            sp.wait_ge(out_stored, 16 * (LAT // P))

        @block.gpsimd
        def _(pool):
            def ada(layer, j, order, k):
                s = order % 2
                wait(pool, ada_used[s], k)
                src = ada_w[layer].rearrange("(k p) f -> p k f", p=P)
                pool.dma_start(ada_slot[s][:], src[:, :, bass.ds(j * P, P)]).then_inc(ada_loaded[s], 16)

            def ada_run(name):
                layer, j0, count, order = ada_parts[name]

                def body(i):
                    for t in range(2):
                        ada(layer, i * 2 + (j0 + t), order + t, order // 2 + i)
                steps(pool, count // 2, body)

            def vectors():
                for la in range(DEPTH):
                    nc.gpsimd.memset(rows_v[2 * la][:], 0.0).then_inc(rows_cleared, 1)
                    nc.gpsimd.memset(rows_v[2 * la + 1][:], 0.0).then_inc(rows_cleared, 1)
                pool.wait_ge(rows_cleared, 2 * DEPTH)
                for la in range(DEPTH):
                    v1, v2, b = rows_v[2 * la], rows_v[2 * la + 1], b_in[la]
                    parts = [(v1[0:MOD_TILES, :], ada_b[la].rearrange("(j p) -> j p", p=P)),
                             (v1[MOD_TILES:MOD_TILES + 6 * KT, :], norm_g[la].rearrange("n (k p) -> (n k) p", p=P)),
                             (v2[T_SMALL:T_SMALL + 1, 0:2 * RANK], b[COL_RANK:COL_RANK + 2 * RANK].rearrange("(a p) -> a p", a=1)),
                             (v2[T_SMALL:T_SMALL + 1, GATE_ROW:GATE_ROW + 4 * C_HEADS],
                              b[COL_GATE:COL_GATE + 4 * C_HEADS].rearrange("(a p) -> a p", a=1)),
                             (v2[V_CONV:V_CONV + 12, :], mlstm_conv[la].rearrange("w (j p) -> (w j) p", p=P)),
                             (v2[V_GLAN:V_GLAN + 2, :], gla_norm[la].rearrange("(j p) -> j p", p=P)),
                             (v2[V_MLN:V_MLN + 2, :], mlstm_norm[la].rearrange("(j p) -> j p", p=P)),
                             (v2[V_BA:V_BA + 2, :], gla_b_alpha[la])]
                    for j, col, m in BIAS_RUNS:
                        parts.append((v2[j:j + m, :], b[col:col + m * P].rearrange("(a p) -> a p", p=P)))
                    for dst, src in parts:
                        pool.dma_start(dst, src).then_inc(rows_loaded, 16)

            def mixer_constants(layer):
                pool.wait_ge(post["ss_done"], 3 * layer + 1)
                nc.gpsimd.memset(w_alpha[:], 0.0).then_inc(mix_cleared, 1)
                nc.gpsimd.memset(f_bias[:], 0.0).then_inc(mix_cleared, 1)
                nc.gpsimd.memset(vm_tok[:, :, :, C_DIM:C_DIM + 1], 1.0).then_inc(mix_cleared, 1)
                pool.wait_ge(mix_cleared, 3 * layer + 3)
                for dst, src in ((rot[:], k_rot), (swap[:], k_swap), (cos[:], k_cos), (sin[:], k_sin),
                                 (band[:], k_band.rearrange("b p k -> p b k")),
                                 (level_mask[:], k_level.rearrange("l p k -> p l k")),
                                 (gate_sel[GATE_ROW:GATE_ROW + 4 * C_HEADS, :, :], k_sel),
                                 (w_alpha[0:RANK, 0, :], gla_w_alpha[layer, 0]),
                                 (w_alpha[RANK:2 * RANK, 1, :], gla_w_alpha[layer, 1]),
                                 (sink[:], attn_sink[layer:layer + 1, :].to_broadcast([P, A_HEADS])),
                                 (f_bias[0:C_HEADS, :], mlstm_f_bias[layer, 0:1, :].rearrange("a h -> h a")),
                                 (f_bias[32:32 + C_HEADS, :], mlstm_f_bias[layer, 1:2, :].rearrange("a h -> h a"))):
                    pool.dma_start(dst, src).then_inc(mix_loaded, 16)

            def gla(layer):
                m, T = mixer, width(layer, 1)
                cum_f, cum_b = gla_cum[:, 0, 0:T], gla_cum[:, 1, 0:T]

                def exponents(lev, half):
                    xk = gla_x[lev % 2][:, 0, 0:T].rearrange("p (n a h) -> p n a h", a=2, h=half)
                    f = cum_f.rearrange("p (n a h) -> p n a h", a=2, h=half)
                    b = cum_b.rearrange("p (n a h) -> p n a h", a=2, h=half)
                    shape = [P, T // (2 * half), half]
                    wait(pool, m["gla_k"], lev - 1)
                    nc.gpsimd.tensor_tensor(xk[:, :, 0, :], f[:, :, 0, half - 1:half].to_broadcast(shape), f[:, :, 0, :],
                                            ALU.subtract).then_inc(m["gla_xk"], 1)
                    nc.gpsimd.tensor_tensor(xk[:, :, 1, :], b[:, :, 1, 0:1].to_broadcast(shape), b[:, :, 1, :],
                                            ALU.subtract).then_inc(m["gla_xk"], 1)

                pool.wait_ge(m["gla_cum_ready"], 4)
                exponents(0, LEVELS[0])
                for lev in range(len(LEVELS)):
                    if lev + 1 < len(LEVELS):
                        exponents(lev + 1, LEVELS[lev + 1])
                    pool.wait_ge(m["gla_ex"], lev + 1)
                    wait(pool, m["gla_mm"], B_HEADS * (lev - 1))
                    nc.gpsimd.tensor_tensor(gla_kq[lev % 2][:, 0, 0:T], proj[:, T_GK, 0:T], gla_x[lev % 2][:, 0, 0:T],
                                            ALU.mult).then_inc(m["gla_k"], 1)

            nc.gpsimd.memset(ones[:], 1.0).then_inc(ones_ready, 1)
            nc.gpsimd.memset(eps_col[:], EPS).then_inc(eps_ready, 1)
            vectors()
            for layer in range(DEPTH):
                if layer == 0:
                    ada_run(("beside", 0, 0))
                    ada_run("down")
                    ada_run(("turn", 0))
                    mixer_constants(0)
                    gla(0)
                    la, j0, count, order = ada_parts["turn", 1]
                    pool.wait_ge(mixer["y_tok_ready"], 2 * (TOK // LAT))
                    for t in range(count):
                        if t == 2:
                            pool.wait_ge(post["ss_done"], 2)
                            for name in MIX:
                                nc.gpsimd.sem_clear(mixer[name])
                        ada(la, j0 + t, order + t, (order + t) // 2)
                    ada_run(("beside", 0, 1))
                else:
                    ada_run(("apart", 1))
                    ada_run(("beside", 1, 0))
                    mixer_constants(1)
                    gla(1)

        @block.scalar
        def _(act):
            def mean_root(T, need, ready, need_count):
                act.wait_ge(need, need_count)
                nc.scalar.activation(rstd[:, 0:T], bank[7][:, 0:T], ACT.Sqrt, bias=eps_col[:], scale=1.0 / DM)\
                    .then_inc(ready, 1)

            def norm_in(layer, q, z, T):
                for k in range(KT):
                    if z == 0:
                        act.wait_ge(x_copied, k + 1)
                    else:
                        act.wait_ge(post["h_added"], KT * (z - 1) + k + 1)
                    wait(act, norm["sq_used"], KT * z + k - 1)
                    nc.scalar.activation(tmp_a[k % 2][:, 0:T], H[:, k, 0:T], ACT.Square).then_inc(norm["sq_ready"], 1)
                mean_root(T, norm["sq_used"], norm["rms_ready"], KT * z + KT)
                for k in range(KT):
                    act.wait_ge(norm["scaled"], KT * z + k + 1)
                    for st in range(T // LAT):
                        part = tmp_b[k % 2][:, st * LAT:(st + 1) * LAT]
                        ins = nc.scalar.activation(part, part, ACT.Identity, bias=mod[layer][:, 3 * q, k, st:st + 1],
                                                   scale=mod[layer][:, 3 * q + 1, k, st:st + 1])
                    ins.then_inc(norm["moded"], 1)
                    act.wait_ge(norm["moded"], KT * z + k + 1)
                    nc.scalar.activation(u_hi[:, k, 0:T], tmp_b[k % 2][:, 0:T], ACT.Copy).then_inc(norm["uhi_ready"], 1)

            def gate_up(layer, q, g, T):
                n0 = first_unit[f"gu{q}", layer]

                def body(i):
                    for j in range(2):
                        f = 2 * i + j
                        ahead_of(split_hi, act, n0, i, 2, j + 1)
                        unit_done(act, n0, i, 2, j)
                        wait(act, gated["prod_ready"], FT * g + f - 1)
                        nc.scalar.activation(tmp_a[j][:, 0:T], bank[2 * j][:, 0:T], ACT.Silu).then_inc(gated["silu_ready"], 1)
                        act.wait_ge(gated["prod_ready"], FT * g + f + 1)
                        nc.scalar.activation(ht_hi[:, f, 0:T], tmp_b[j][:, 0:T], ACT.Copy).then_inc(gated["hthi_ready"], 1)
                steps(act, FT // 2, body)

            def post_tile(dst, z, t, b, T):
                nc.scalar.activation(dst[:, t, 0:T], bank[4 + b][:, 0:T], ACT.Copy).then_inc(post["y_ready"], 1)
                wait(act, post["ysq_added"], KT * z + t - 1)
                nc.scalar.activation(tmp_a[b][:, 0:T], bank[4 + b][:, 0:T], ACT.Square).then_inc(post["ysq_ready"], 1)

            def down(layer, q, z, T):
                n0 = first_unit[f"dn{q}", layer]

                def body(i):
                    for t in range(2):
                        for j in range(2):
                            ahead = 2 * t + j + 1
                            ahead_of(split_hi, act, n0, i, 4, ahead)
                        unit_done(act, n0, i, 4, 2 * t + 1)
                        post_tile(Y_ffn, z, 2 * i + t, t, T)
                steps(act, KT // 2, body)
                mean_root(T, post["ss_done"], post["ss_rms"], z + 1)

            def project(layer, m):
                n0 = first_unit["in", layer]
                for t in range(N_PROJ):
                    if t % 2 == 0:
                        split_hi(act, n0 + t // 2 + 1)
                    T = width(layer, 1) if t < LAT_ONLY else TOK
                    rows = P if t < T_SMALL else GATE_ROW + 4 * C_HEADS
                    unit_done(act, n0, 0, 2, t // 2)
                    nc.scalar.activation(proj[0:rows, t, 0:T], bank[t % 4][0:rows, 0:T], ACT.Identity,
                                         bias=vec2[layer][0:rows, t:t + 1]).then_inc(m["proj_ready"], 1)

            def attention(layer, m, NQ):
                for tt in range(TT):
                    act.wait_ge(m["v_turned"], tt + 1)
                    nc.scalar.activation(v_tok[:, tt, :], bank[3 + tt][:, 0:3 * P], ACT.Copy).then_inc(m["v_ready"], 1)
                act.wait_ge(m["swap_done"], 1)
                nc.scalar.activation(k_swapped[:], bank[1][:], ACT.Copy).then_inc(m["swap_ready"], 1)
                N = A_HEADS * NQ

                def turned(i):
                    qb = i // A_HEADS
                    W = TOK if qb < 2 else CTX
                    act.wait_ge(m["turned"], i + 1)
                    wait(act, m["pv_done"], i - 1)
                    nc.scalar.activation(probs_t[i % 2][:].rearrange("p a b -> p (a b)")[:, 0:W], bank[4 + i % 2][:, 0:W],
                                         ACT.Copy).then_inc(m["pt_ready"], 1)

                for i in range(N):
                    qb = i // A_HEADS
                    W = TOK if qb < 2 else CTX
                    act.wait_ge(m["max_step"], 2 * i + 2)
                    wait(act, m["turned"], i - 2)
                    nc.scalar.activation(probs[i % 3][:, 0:W], bank[(i % 2) * 2 + i // 2 % 2][:, 0:W], ACT.Exp,
                                         bias=neg_max[:, i:i + 1], scale=A_DIM ** -0.5,
                                         accum_out=row_sum[:, i:i + 1]).then_inc(m["exp_done"], 1)
                    if i >= 1:
                        turned(i - 1)
                turned(N - 1)
                act.wait_ge(m["sink_step"], 2)
                nc.scalar.activation(sink_exp[:, 0:N], sink_exp[:, 0:N], ACT.Exp).then_inc(m["sink_done"], 1)

            def gla(layer, m, T):
                z = gla_x[0][:].rearrange("p a t -> p (a t)")
                act.wait_ge(m["gla_z_ready"], 2)
                nc.scalar.activation(z, gla_z[:].rearrange("p a t -> p (a t)"), ACT.Abs).then_inc(m["gla_act"], 1)
                act.wait_ge(m["gla_act"], 1)
                nc.scalar.activation(z, z, ACT.Exp, scale=-1.0).then_inc(m["gla_act"], 1)
                act.wait_ge(m["gla_act"], 2)
                nc.scalar.activation(z, z, ACT.Ln, bias=1.0).then_inc(m["gla_act"], 1)

                def put(lev):
                    dst = gla_pair if lev == 0 else gla_diag
                    for h in range(B_HEADS):
                        act.wait_ge(m["gla_mm"], B_HEADS * lev + h + 1)
                        nc.scalar.activation(dst[:, h, :, :].rearrange("p a b -> p (a b)")[:, 0:T],
                                             bank[(lev % 2) * 4 + h][:, 0:T], ACT.Copy).then_inc(m["gla_put_act"], 1)

                for lev in range(len(LEVELS)):
                    act.wait_ge(m["gla_xk"], 2 * lev + 2)
                    act.wait_ge(m["gla_xq"], 2 * lev + 2)
                    nc.scalar.activation(gla_x[lev % 2][:, :, 0:T], gla_x[lev % 2][:, :, 0:T], ACT.Exp,
                                         scale=1.0 / TAU).then_inc(m["gla_ex"], 1)
                    if lev in (1, 2):
                        put(lev - 1)
                act.wait_ge(m["gla_bt"], 2)
                act.wait_ge(m["gla_k"], len(LEVELS))
                act.wait_ge(m["gla_qs"], len(LEVELS))
                for d in range(2):
                    nc.scalar.activation(gla_x[0][:, d, 0:LAT], gla_cum[:, d, 0:LAT], ACT.Exp, scale=1.0 / TAU)\
                        .then_inc(m["gla_cx"], 1)
                    nc.scalar.activation(gla_x[0][:, d, LAT:TOK], gla_cum[:, d, LAT:TOK], ACT.Exp, scale=-1.0 / TAU,
                                         bias=bt_col[:, d:d + 1]).then_inc(m["gla_cx"], 1)
                for h in range(B_HEADS):
                    act.wait_ge(m["gla_cmm"], h + 1)
                    nc.scalar.activation(gla_cross[:, h, :, :].rearrange("p a b -> p (a b)"), bank[4 + h][:], ACT.Copy)\
                        .then_inc(m["gla_cput"], 1)
                gates_and_conv(layer, m, T)
                head_norm(m, "gla_ln", "gla_sqrt", T // LAT)

            def head_norm(m, ln, root, streams):
                for g in range(streams):
                    act.wait_ge(m[ln], 6 * g + 5)
                    nc.scalar.activation(ln_s[:, 2, 8 * g:8 * g + 8], ln_s[:, 1, 8 * g:8 * g + 8], ACT.Sqrt,
                                         bias=eps_col[:], scale=1.0 / 64).then_inc(m[root], 1)

            def mlstm(layer, m, T):
                act.wait_ge(m["gate_row"], 1)
                nc.scalar.activation(g_b[:], g_f[:], ACT.Abs).then_inc(m["gate_act"], 1)
                act.wait_ge(m["gate_act"], 1)
                nc.scalar.activation(g_b[:], g_b[:], ACT.Exp, scale=-1.0).then_inc(m["gate_act"], 1)
                act.wait_ge(m["gate_act"], 2)
                nc.scalar.activation(g_b[:], g_b[:], ACT.Ln, bias=1.0).then_inc(m["gate_act"], 1)
                act.wait_ge(m["gate_turned"], 2)
                nc.scalar.activation(a_col[:].rearrange("p a b -> p (a b)"), bank[6][:, 0:TT * 64], ACT.Copy)\
                    .then_inc(m["gate_col"], 1)
                nc.scalar.activation(em_col[:].rearrange("p a b -> p (a b)"), bank[6][:, TT * 64:2 * TT * 64], ACT.Exp,
                                     scale=-1.0).then_inc(m["gate_col"], 1)
                act.wait_ge(m["gate_col"], 2)
                for x in range(2 * C_HEADS):
                    h, d = x // 2, x % 2
                    r = 32 * d + h
                    W = w_c[x % 2]
                    wait(act, m["num_done"], x - 1)
                    act.wait_ge(m["g_done"], x + 1)
                    act.wait_ge(m["xg_ready"], x + 1)
                    last = None
                    for grp in range(T // LAT):
                        for si in range(2):
                            tt = 2 * grp + si
                            last = nc.scalar.activation(W[:, grp, si, si * P:(si + 1) * P], xg[x % 2][:, tt, :], ACT.Exp,
                                                        bias=a_col[:, tt, r:r + 1])
                        si = d
                        ti = 1 - d
                        last = nc.scalar.activation(W[:, grp, si, ti * P:(ti + 1) * P],
                                                    bank[6][:, grp * LAT + ti * P:grp * LAT + (ti + 1) * P], ACT.Exp,
                                                    bias=a_col[:, 2 * grp + si, r:r + 1], scale=-1.0)
                    for j in range(2):
                        last = nc.scalar.activation(W[:, 2, j, :], bank[6][:, 0:LAT], ACT.Exp,
                                                    bias=a_col[:, 2 + j, r:r + 1], scale=-1.0)
                    last.then_inc(m["w_ready"], 1)
                head_norm(m, "ml_ln", "ml_sqrt", T // LAT)

            def gates_and_conv(layer, m, T):
                act.wait_ge(m["conv"], 12)
                for j in range(4):
                    Tj = T if j == 0 else TOK
                    nc.scalar.activation(qk_conv[:, j, 0:Tj], qk_conv[:, j, 0:Tj], ACT.Silu).then_inc(m["qk_ready"], 1)
                nc.scalar.activation(proj[:, T_GG:T_GG + 2, 0:T], proj[:, T_GG:T_GG + 2, 0:T], ACT.Silu).then_inc(m["qk_ready"], 1)
                nc.scalar.activation(proj[:, T_OG:T_OG + 2, 0:T], proj[:, T_OG:T_OG + 2, 0:T], ACT.Sigmoid).then_inc(m["qk_ready"], 1)

            def turn_y(layer, m, T):
                for f in range(KT):
                    if f < 4:
                        act.wait_ge(m["yt_turned"], f + 1)
                        src = bank[f][:, 0:T]
                    else:
                        act.wait_ge(m["yt_full"], f - 3)
                        src = tmp_b[f % 2][:, 0:T]
                    nc.scalar.activation(u_hi[:, f, 0:T], src, ACT.Copy).then_inc(m["yt_hi"], 1)

            def project_out(layer, z, T):
                n0 = first_unit["out", layer]
                for t in range(KT):
                    if t % 2 == 0:
                        split_hi(act, n0 + t // 2 + 1)
                    unit_done(act, n0, 0, 2, t // 2)
                    post_tile(Y_mix, z, t, t % 2, T)
                mean_root(T, post["ss_done"], post["ss_rms"], z + 1)

            act.wait_ge(c_loaded, 48)
            nc.scalar.activation(rows_c[:], rows_c[:], ACT.Silu).then_inc(c_silu, 1)
            act.wait_ge(c_turned, 1)
            nc.scalar.activation(silu_c[:], bank[0][:, 0:2 * KT], ACT.Copy).then_inc(c_ready, 1)
            for k in range(KT):
                act.wait_ge(x_turned, k + 1)
                nc.scalar.activation(H[:, k, :], bank[k % 4][:], ACT.Copy).then_inc(x_copied, 1)
            act.wait_ge(rows_turned, 2 * DEPTH)
            for la in range(DEPTH):
                nc.scalar.activation(vec1[la][:], bank[4][:, la * P:la * P + MOD_TILES + 6 * KT], ACT.Copy).then_inc(vec_ready, 1)
                nc.scalar.activation(vec2[la][:], bank[4][:, (2 + la) * P:(2 + la) * P + N_VEC2], ACT.Copy).then_inc(vec_ready, 1)
            split_hi(act, 0)
            for layer in range(DEPTH):
                m, z = mixer, 3 * layer
                norm_in(layer, 0, z, TOK)
                gate_up(layer, 0, 2 * layer, TOK)
                down(layer, 0, z, TOK)
                norm_in(layer, 1, z + 1, TOK)
                project(layer, m)
                T = width(layer, 1)
                attention(layer, m, T // P)
                gla(layer, m, T)
                mlstm(layer, m, T)
                turn_y(layer, m, T)
                project_out(layer, z + 1, T)
                norm_in(layer, 2, z + 2, T)
                gate_up(layer, 1, 2 * layer + 1, T)
                down(layer, 1, z + 2, T)
            for t in range(LAT // P):
                for g in range(2):
                    act.wait_ge(out_turned, 2 * t + g + 1)
                    nc.scalar.activation(Y_ffn[:, 2 * t + g, :], bank[2 * t + g][:], ACT.Copy).then_inc(out_copied, 1)

        @block.vector
        def _(dve):
            def invert(need, need_count, ready, ready_count, T):
                dve.wait_ge(need, need_count)
                nc.vector.reciprocal(rstd[:, 0:T], rstd[:, 0:T]).then_inc(ready, 1)
                dve.wait_ge(ready, ready_count)

            def norm_in(layer, q, z, T):
                invert(norm["rms_ready"], z + 1, norm["rstd_ready"], z + 1, T)

                def low(k):
                    dve.wait_ge(norm["uhi_ready"], KT * z + k + 1)
                    nc.vector.tensor_tensor(u_lo[:, k, 0:T], tmp_b[k % 2][:, 0:T], u_hi[:, k, 0:T].bitcast(F32),
                                            ALU.subtract).then_inc(norm["u_ready"], 1)

                for k in range(KT):
                    wait(dve, norm["u_ready"], KT * z + k - 1)
                    nc.vector.tensor_tensor(tmp_b[k % 2][:, 0:T], H[:, k, 0:T], rstd[:, 0:T], ALU.mult)\
                        .then_inc(norm["scaled"], 1)
                    if k >= 1:
                        low(k - 1)
                low(KT - 1)

            def gate_up(layer, q, g, T):
                n0 = first_unit[f"gu{q}", layer]

                def body(i):
                    for j in range(2):
                        f = 2 * i + j
                        ahead_of(split_lo, dve, n0, i, 2, j + 1)
                        dve.wait_ge(gated["silu_ready"], FT * g + f + 1)
                        wait(dve, gated["ht_ready"], FT * g + f - 1)
                        nc.vector.tensor_tensor(tmp_b[j][:, 0:T], bank[2 * j + 1][:, 0:T], tmp_a[j][:, 0:T],
                                                ALU.mult).then_inc(gated["prod_ready"], 1)
                        dve.wait_ge(gated["hthi_ready"], FT * g + f + 1)
                        nc.vector.tensor_tensor(ht_lo[:, f, 0:T], tmp_b[j][:, 0:T], ht_hi[:, f, 0:T].bitcast(F32),
                                                ALU.subtract).then_inc(gated["ht_ready"], 1)
                steps(dve, FT // 2, body)

            def add_squares(z, t, b, T, first):
                dve.wait_ge(post["ysq_ready"], KT * z + t + 1)
                if first:
                    ins = nc.vector.tensor_copy(sq_sum[:, 0:T], tmp_a[b][:, 0:T])
                else:
                    dve.wait_ge(post["ysq_added"], KT * z + t)
                    ins = nc.vector.tensor_tensor(sq_sum[:, 0:T], sq_sum[:, 0:T], tmp_a[b][:, 0:T], ALU.add)
                ins.then_inc(post["ysq_added"], 1)

            def post_norm(layer, q, z, T, Y):
                invert(post["ss_rms"], z + 1, post["ss_rstd"], z + 1, T)

                def scale(k):
                    wait(dve, post["h_added"], KT * z + k - 1)
                    nc.vector.tensor_tensor(tmp_b[k % 2][:, 0:T], Y[:, k, 0:T], rstd[:, 0:T], ALU.mult)\
                        .then_inc(post["y_scaled"], 1)

                scale(0)
                for k in range(KT):
                    if k + 1 < KT:
                        scale(k + 1)
                    dve.wait_ge(post["y_scaled"], KT * z + k + 1)
                    for st in range(T // LAT):
                        cols = slice(st * LAT, (st + 1) * LAT)
                        ins = nc.vector.scalar_tensor_tensor(H[:, k, cols], tmp_b[k % 2][:, cols],
                                                             mod[layer][:, 3 * q + 2, k, st:st + 1], H[:, k, cols],
                                                             ALU.mult, ALU.add)
                    ins.then_inc(post["h_added"], 1)

            def down(layer, q, z, T):
                n0 = first_unit[f"dn{q}", layer]

                def body(i):
                    for t in range(2):
                        for j in range(2):
                            ahead = 2 * t + j + 1
                            ahead_of(split_lo, dve, n0, i, 4, ahead)
                        add_squares(z, 2 * i + t, t, T, isinstance(i, int) and i + t == 0)
                steps(dve, KT // 2, body)

            def modulation(layer, m0, m1, done_tiles, before):
                dve.wait_ge(first_used, FIRST_TILES)
                for s in range(2):
                    wait(dve, ada_used[s], done_tiles // 2)
                dve.wait_ge(vec_ready, 2 * DEPTH)
                n = [before]

                def step(ins):
                    n[0] += 1
                    ins.then_inc(mod_step, 1)

                acc = mod_acc.rearrange("p (m k s) -> p m k s", k=KT, s=2)
                for mm in range(m0, m1):
                    bias = vec1[layer][:, mm * KT:(mm + 1) * KT].unsqueeze(2).to_broadcast([P, KT, 2])
                    step(nc.vector.tensor_tensor(mod[layer][:, mm, :, :], acc[:, mm, :, :], bias, ALU.add))
                dve.wait_ge(mod_step, n[0])
                for mm in range(m0, m1):
                    q, kind = mm // 3, mm % 3
                    if kind == 0:
                        continue
                    row = MOD_TILES + (2 * q + kind - 1) * KT
                    gain = vec1[layer][:, row:row + KT].unsqueeze(2).to_broadcast([P, KT, 2])
                    this = mod[layer][:, mm, :, :]
                    number, op = (1.0, ALU.add) if kind == 1 else ((1.0 if q == 1 else FFN_RES), ALU.mult)
                    step(nc.vector.scalar_tensor_tensor(this, this, number, gain, op, ALU.mult))
                dve.wait_ge(mod_step, n[0])
                return n[0]

            def attention(layer, m, NQ):
                for g in range(2):
                    dve.wait_ge(m["v_turned"], TT + g + 1)
                    nc.vector.tensor_copy(vm_tok[:, 2 * g:2 * g + 2, :, 0:C_DIM],
                                          bank[[7, 2][g]][:].rearrange("p (t h d) -> p t h d", t=2, d=C_DIM))\
                        .then_inc(m["vm_ready"], 1)
                    if g == 0:
                        rope(layer, m)
                dve.wait_ge(mix_loaded, 16 * 12 * (layer + 1))
                nc.vector.tensor_scalar(neg_sink[:], sink[:], -1.0, None, ALU.mult).then_inc(m["sink_step"], 1)
                dve.wait_ge(m["sink_step"], 1)
                N = A_HEADS * NQ

                def put(i):
                    qb, h = i // A_HEADS, i % A_HEADS
                    dve.wait_ge(m["pv_done"], i + 1)
                    nc.vector.tensor_copy(y_tok[:, qb, h * A_DIM:(h + 1) * A_DIM], bank[6 + i % 2][:, 0:A_DIM])\
                        .then_inc(m["o_ready"], 1)

                for i in range(N):
                    qb, h = i // A_HEADS, i % A_HEADS
                    W = TOK if qb < 2 else CTX
                    dve.wait_ge(m["score"], i + 1)
                    nc.vector.tensor_reduce(row_max[:, i:i + 1], bank[(i % 2) * 2 + i // 2 % 2][:, 0:W], AX_X,
                                            ALU.max).then_inc(m["max_step"], 1)
                    dve.wait_ge(m["max_step"], 2 * i + 1)
                    nc.vector.tensor_scalar(neg_max[:, i:i + 1], row_max[:, i:i + 1], -A_DIM ** -0.5, neg_sink[:, h:h + 1],
                                            ALU.mult, ALU.min).then_inc(m["max_step"], 1)
                    if i >= 3:
                        put(i - 3)
                for i in range(N - 3, N):
                    put(i)
                dve.wait_ge(m["max_step"], 2 * N)
                by_head = neg_max[:, 0:N].rearrange("p (q h) -> p q h", h=A_HEADS)
                nc.vector.tensor_tensor(sink_exp[:, 0:N].rearrange("p (q h) -> p q h", h=A_HEADS), by_head,
                                        sink[:].unsqueeze(1).to_broadcast([P, NQ, A_HEADS]), ALU.add).then_inc(m["sink_step"], 1)
                dve.wait_ge(m["sink_done"], 1)
                nc.vector.tensor_tensor(row_sum[:, 0:N], row_sum[:, 0:N], sink_exp[:, 0:N], ALU.add).then_inc(m["sink_step"], 1)
                dve.wait_ge(m["sink_step"], 3)
                nc.vector.reciprocal(row_sum[:, 0:N], row_sum[:, 0:N]).then_inc(m["sink_step"], 1)
                dve.wait_ge(m["sink_step"], 4)
                dve.wait_ge(m["o_ready"], N)
                for qb in range(NQ):
                    y = y_tok[:, qb, 0:A_HEADS * A_DIM].rearrange("p (h d) -> p h d", d=A_DIM)
                    nc.vector.tensor_tensor(y, y, row_sum[:, qb * A_HEADS:(qb + 1) * A_HEADS].unsqueeze(2)
                                            .to_broadcast([P, A_HEADS, A_DIM]), ALU.mult).then_inc(m["sink_step"], 1)
                dve.wait_ge(m["sink_step"], 4 + NQ)

            def rope(layer, m):
                dve.wait_ge(mix_loaded, 16 * 12 * (layer + 1))
                pieces = [(0, T_Q, 2), (1, T_Q + 2, 2), (2, T_K, 1)]
                count = 0
                for b, t, n in pieces:
                    dve.wait_ge(m["rot_done"], b + 1)
                    shape = [P, n, LAT]
                    nc.vector.tensor_tensor(rope_tmp[:, 2 * b:2 * b + n, :], bank[b][:, 0:n * LAT].rearrange("p (a t) -> p a t", a=n),
                                            sin[:].unsqueeze(1).to_broadcast(shape), ALU.mult).then_inc(m["rope_step"], 1)
                    nc.vector.tensor_tensor(proj[:, t:t + n, 0:LAT], proj[:, t:t + n, 0:LAT],
                                            cos[:].unsqueeze(1).to_broadcast(shape), ALU.mult).then_inc(m["rope_step"], 1)
                    count += 2
                dve.wait_ge(m["rope_step"], count)
                for b, t, n in pieces:
                    nc.vector.tensor_tensor(proj[:, t:t + n, 0:LAT], proj[:, t:t + n, 0:LAT], rope_tmp[:, 2 * b:2 * b + n, :],
                                            ALU.add).then_inc(m["rope_step"], 1)

            def gla(layer, m, T):
                for d in range(2):
                    dve.wait_ge(m["gla_z_mm"], d + 1)
                    nc.vector.tensor_scalar(gla_z[:, d, :], bank[d][:], vec2[layer][:, V_BA + d:V_BA + d + 1], None,
                                            ALU.add).then_inc(m["gla_z_ready"], 1)
                dve.wait_ge(m["gla_act"], 3)
                z = gla_z[:].rearrange("p a t -> p (a t)")
                nc.vector.scalar_tensor_tensor(z, z, 0.0, gla_x[0][:].rearrange("p a t -> p (a t)"), ALU.min,
                                               ALU.subtract).then_inc(m["gla_la"], 1)
                dve.wait_ge(m["gla_la"], 1)
                one = ones[:, 0:1].to_broadcast([P, LAT])
                for st in range(2):
                    cols = slice(st * LAT, (st + 1) * LAT)
                    nc.vector.tensor_tensor_scan(gla_cum[:, 0, cols], one, gla_z[:, 0, cols], 0.0, ALU.mult, ALU.add)\
                        .then_inc(m["gla_cum_ready"], 1)
                    nc.vector.tensor_tensor_scan(gla_cum[:, 1, cols][:, ::-1], one, gla_z[:, 1, cols][:, ::-1], 0.0,
                                                 ALU.mult, ALU.add).then_inc(m["gla_cum_ready"], 1)
                nc.vector.tensor_scalar(proj[:, T_GQ, 0:T], proj[:, T_GQ, 0:T], B_DK ** -0.5, None, ALU.mult).then_inc(m["gla_q"], 1)
                dve.wait_ge(m["gla_cum_ready"], 4)
                nc.vector.tensor_scalar(bt_col[:, 0:1], gla_cum[:, 0, TOK - 1:TOK], 1.0 / TAU, None, ALU.mult).then_inc(m["gla_bt"], 1)
                nc.vector.tensor_scalar(bt_col[:, 1:2], gla_cum[:, 1, LAT:LAT + 1], 1.0 / TAU, None, ALU.mult).then_inc(m["gla_bt"], 1)
                cum_f, cum_b = gla_cum[:, 0, 0:T], gla_cum[:, 1, 0:T]

                def exponents(lev):
                    half = LEVELS[lev]
                    xq = gla_x[lev % 2][:, 1, 0:T].rearrange("p (n a h) -> p n a h", a=2, h=half)
                    f = cum_f.rearrange("p (n a h) -> p n a h", a=2, h=half)
                    b = cum_b.rearrange("p (n a h) -> p n a h", a=2, h=half)
                    shape = [P, T // (2 * half), half]
                    wait(dve, m["gla_qs"], lev - 1)
                    nc.vector.tensor_tensor(xq[:, :, 1, :], f[:, :, 1, :], f[:, :, 0, half - 1:half].to_broadcast(shape),
                                            ALU.subtract).then_inc(m["gla_xq"], 1)
                    nc.vector.tensor_tensor(xq[:, :, 0, :], b[:, :, 0, :], b[:, :, 1, 0:1].to_broadcast(shape),
                                            ALU.subtract).then_inc(m["gla_xq"], 1)

                def put(lev):
                    for h in range(B_HEADS):
                        dve.wait_ge(m["gla_mm"], B_HEADS * lev + h + 1)
                        dve.wait_ge(m["gla_put_act"], B_HEADS + h + 1)
                        wait(dve, m["gla_put"], B_HEADS * (lev - 3) + h + 1)
                        nt = T // P
                        nc.vector.copy_predicated(gla_diag[:, h, 0:nt, :],
                                                  level_mask[:, lev - 2, :].bitcast(U32).unsqueeze(1).to_broadcast([P, nt, P]),
                                                  bank[(lev % 2) * 4 + h][:, 0:T].rearrange("p (a b) -> p a b", b=P))\
                            .then_inc(m["gla_put"], 1)

                dve.wait_ge(m["gla_q"], 1)
                exponents(0)
                for lev in range(len(LEVELS)):
                    if lev + 1 < len(LEVELS):
                        exponents(lev + 1)
                    dve.wait_ge(m["gla_ex"], lev + 1)
                    wait(dve, m["gla_mm"], B_HEADS * (lev - 1))
                    nc.vector.tensor_tensor(gla_kq[lev % 2][:, 1, 0:T], proj[:, T_GQ, 0:T], gla_x[lev % 2][:, 1, 0:T],
                                            ALU.mult).then_inc(m["gla_qs"], 1)
                    if lev >= 3:
                        put(lev - 1)
                last = len(LEVELS)
                dve.wait_ge(m["gla_mm"], B_HEADS * (last - 1))
                nc.vector.tensor_scalar(gla_kq[last % 2][:, 1, 0:T], proj[:, T_GQ, 0:T], 2.0, None, ALU.mult).then_inc(m["gla_qs"], 1)
                put(last - 1)
                put(last)
                dve.wait_ge(m["gla_cx"], 4)
                kq = gla_kq[0]
                for cols, tile in ((slice(0, LAT), T_GQ), (slice(LAT, TOK), T_GK)):
                    nc.vector.tensor_tensor(kq[:, :, cols], gla_x[0][:, :, cols],
                                            proj[:, tile, cols].unsqueeze(1).to_broadcast([P, 2, LAT]), ALU.mult)\
                        .then_inc(m["gla_cqk"], 1)
                convolution(layer, m, T)
                head_norm(m, "gla_ln", "gla_sqrt", [bank[g][:].rearrange("p (n d) -> p n d", d=64) for g in range(T // LAT)],
                          m["gla_o"], 512)

            def head_norm(m, ln, root, sources, ready, at):
                n = 0
                for g, src in enumerate(sources):
                    if ready is not None:
                        dve.wait_ge(ready, g + 1)
                    G = slice(8 * g, 8 * g + 8)
                    shape = [P, 8, 64]

                    def bc(row):
                        return ln_s[:, row, G].unsqueeze(2).to_broadcast(shape)

                    y = y_tok[:, 2 * g:2 * g + 2, at:at + 256].rearrange("p t (h d) -> p t h d", d=64)
                    nc.vector.tensor_reduce(ln_s[:, 0, G], src, AX_X, ALU.add).then_inc(m[ln], 1)
                    dve.wait_ge(m[ln], n + 1)
                    nc.vector.tensor_scalar(ln_s[:, 3, G], ln_s[:, 0, G], -1.0 / 64, None, ALU.mult).then_inc(m[ln], 1)
                    dve.wait_ge(m[ln], n + 2)
                    nc.vector.tensor_tensor(ln_c[:, G, :], src, bc(3), ALU.add).then_inc(m[ln], 1)
                    dve.wait_ge(m[ln], n + 3)
                    nc.vector.tensor_tensor(ln_sq[:, G, :], ln_c[:, G, :], ln_c[:, G, :], ALU.mult).then_inc(m[ln], 1)
                    dve.wait_ge(m[ln], n + 4)
                    nc.vector.tensor_reduce(ln_s[:, 1, G], ln_sq[:, G, :], AX_X, ALU.add).then_inc(m[ln], 1)
                    dve.wait_ge(m[root], g + 1)
                    nc.vector.reciprocal(ln_s[:, 0, G], ln_s[:, 2, G]).then_inc(m[ln], 1)
                    n += 6
                    dve.wait_ge(m[ln], n)
                    for t in range(2):
                        four = slice(8 * g + 4 * t, 8 * g + 4 * t + 4)
                        ins = nc.vector.tensor_tensor(y[:, t], ln_c[:, four, :],
                                                ln_s[:, 0, four].unsqueeze(2).to_broadcast([P, 4, 64]), ALU.mult)
                    ins.then_inc(m["y_tok_ready"], 1)

            def convolution(layer, m, T):
                def view(t, n):
                    return t.rearrange("p (s t) -> p s t", t=LAT) if n == TOK else t.unsqueeze(1)

                for tap in (1, 0, 2):
                    for j in range(4):
                        Tj = T if j == 0 else TOK
                        w = vec2[layer][:, V_CONV + 4 * tap + j:V_CONV + 4 * tap + j + 1]
                        dst, src = view(qk_conv[:, j, 0:Tj], Tj), view(proj[:, T_MQ + j, 0:Tj], Tj)
                        if tap == 1:
                            ins = nc.vector.tensor_scalar(dst, src, w, None, ALU.mult)
                        else:
                            dve.wait_ge(m["conv"], (4 if tap == 0 else 8) - 4 + j + 1)
                            d, s = (dst[:, :, 1:LAT], src[:, :, 0:LAT - 1]) if tap == 0 else (dst[:, :, 0:LAT - 1], src[:, :, 1:LAT])
                            ins = nc.vector.scalar_tensor_tensor(d, s, w, d, ALU.mult, ALU.add)
                        ins.then_inc(m["conv"], 1)

            def mlstm(layer, m, T):
                NQ = T // P
                dve.wait_ge(m["y_tok_ready"], T // LAT)
                dve.wait_ge(m["gate_mm"], 2)
                nc.vector.tensor_scalar(g_f[:], bank[6][0:64, :], f_bias[:], None, ALU.add).then_inc(m["gate_row"], 1)
                nc.vector.tensor_copy(g_i[:], bank[7][0:64, :]).then_inc(m["gate_row"], 1)
                dve.wait_ge(m["gate_act"], 3)
                dve.wait_ge(m["gate_row"], 2)
                nc.vector.scalar_tensor_tensor(g_f[:], g_f[:], 0.0, g_b[:], ALU.min, ALU.subtract).then_inc(m["gate_row"], 1)
                dve.wait_ge(m["gate_row"], 3)
                nc.vector.memset(g_b[:], 0.0).then_inc(m["gate_row"], 1)
                nc.vector.memset(g_max[:], 0.0).then_inc(m["gate_row"], 1)
                dve.wait_ge(m["gate_row"], 5)

                def scans(out_t, in_t, op0, base):
                    for part in range(2):
                        for d in range(2):
                            r = slice(32 * d, 32 * d + C_HEADS)
                            cols = slice(LAT, TOK) if part == 0 else slice(0, LAT)
                            o, x = out_t[r, cols], in_t[r, cols]
                            end = TOK - 1 if d == 0 else LAT
                            first = 0.0 if part == 0 else out_t[r, end:end + 1]
                            one = ones[r, 0:1].to_broadcast([C_HEADS, LAT])
                            if d == 1:
                                o, x = o[:, ::-1], x[:, ::-1]
                            if op0 == ALU.mult:
                                ins = nc.vector.tensor_tensor_scan(o, one, x, first, ALU.mult, ALU.add)
                            else:
                                ins = nc.vector.tensor_tensor_scan(o, x, x, first, ALU.max, ALU.max)
                            ins.then_inc(m["gate_row"], 1)
                        dve.wait_ge(m["gate_row"], base + 2 * part + 2)

                scans(g_b, g_f, ALU.mult, 5)
                nc.vector.tensor_tensor(g_i[:], g_i[:], g_b[:], ALU.subtract).then_inc(m["gate_row"], 1)
                dve.wait_ge(m["gate_row"], 10)
                scans(g_max, g_i, ALU.max, 10)
                nc.vector.tensor_tensor(g_b[:], g_b[:], g_max[:], ALU.add).then_inc(m["gate_row"], 1)
                dve.wait_ge(m["gate_col"], 2)
                dve.wait_ge(mix_loaded, 16 * 12 * (layer + 1))

                def heads_done(x):
                    h, d = x // 2, x % 2
                    num = bank[7][:, 0:NQ * (C_DIM + 1)].rearrange("p (t e) -> p t e", e=C_DIM + 1)
                    dve.wait_ge(m["num_done"], x + 1)
                    n = 5 * x
                    den = num[:, :, C_DIM]

                    def step(ins):
                        nonlocal n
                        n += 1
                        ins.then_inc(m["hid_step"], 1)
                        dve.wait_ge(m["hid_step"], n)

                    step(nc.vector.scalar_tensor_tensor(c_den[:, 0:NQ], den, -1.0, em_col[:, 0:NQ, 32 * d + h],
                                                        ALU.mult, ALU.max))
                    step(nc.vector.tensor_tensor(c_den[:, 0:NQ], den, c_den[:, 0:NQ], ALU.max))
                    step(nc.vector.reciprocal(c_den[:, 0:NQ], c_den[:, 0:NQ]))
                    rec = c_den[:, 0:NQ].unsqueeze(2).to_broadcast([P, NQ, C_DIM])
                    dst = hid[:, 0:NQ, h, :] if d == 0 else hid_tmp[:, 0:NQ, :]
                    step(nc.vector.tensor_tensor(dst, num[:, :, 0:C_DIM], rec, ALU.mult))
                    if d == 1:
                        step(nc.vector.tensor_tensor(hid[:, 0:NQ, h, :], hid[:, 0:NQ, h, :], hid_tmp[:, 0:NQ, :], ALU.add))
                    else:
                        step(nc.vector.memset(hid_tmp[:, 0:NQ, 0:1], 0.0))

                for x in range(2 * C_HEADS):
                    h, d = x // 2, x % 2
                    dve.wait_ge(m["g_done"], x + 1)
                    wait(dve, m["w_ready"], x - 1)
                    nc.vector.scalar_tensor_tensor(xg[x % 2][:, 0:NQ, :], bank[6][:, 0:T].rearrange("p (a b) -> p a b", b=P), -1.0,
                                                   band[:, 1 - d, :].unsqueeze(1).to_broadcast([P, NQ, P]),
                                                   ALU.mult, ALU.add).then_inc(m["xg_ready"], 1)
                    dve.wait_ge(m["w_ready"], x + 1)
                    dve.wait_ge(m["kq_done"], h + 1)
                    W, b0 = w_c[x % 2], 3 * (h % 2)
                    for grp in range(T // LAT):
                        src = bank[b0 + 2 * grp][:].rearrange("p (s t) -> p s t", s=2)
                        for si in range(2):
                            full = si == d
                            cols = slice(0, LAT) if full else slice(si * P, (si + 1) * P)
                            nc.vector.scalar_tensor_tensor(W[:, grp, si, cols], src[:, si, cols], C_DIM ** -0.5,
                                                           W[:, grp, si, cols], ALU.mult, ALU.mult)
                    nc.vector.scalar_tensor_tensor(W[:, 2, :, :], bank[b0 + 1][:].rearrange("p (s t) -> p s t", s=2),
                                                   C_DIM ** -0.5, W[:, 2, :, :], ALU.mult, ALU.mult).then_inc(m["p_ready"], 1)
                    if x >= 1:
                        heads_done(x - 1)
                heads_done(2 * C_HEADS - 1)
                head_norm(m, "ml_ln", "ml_sqrt",
                          [hid[:, 2 * g:2 * g + 2, :, :].rearrange("p t h d -> p (t h) d") for g in range(T // LAT)], None, 768)

            def turn_y(layer, m, T):
                def low(f):
                    dve.wait_ge(m["yt_hi"], f + 1)
                    src = bank[f][:, 0:T] if f < 4 else tmp_b[f % 2][:, 0:T]
                    nc.vector.tensor_tensor(u_lo[:, f, 0:T], src, u_hi[:, f, 0:T].bitcast(F32), ALU.subtract)\
                        .then_inc(m["yt_ready"], 1)

                for f in range(4, KT):
                    dve.wait_ge(m["yt_turned"], f + 1)
                    if f >= 6:
                        dve.wait_ge(m["yt_ready"], 4 + f - 6 + 1)
                    gain = V_GLAN + f - 4
                    gate = T_GG + f - 4
                    nc.vector.scalar_tensor_tensor(tmp_b[f % 2][:, 0:T], bank[f][:, 0:T], vec2[layer][:, gain:gain + 1],
                                                   proj[:, gate, 0:T], ALU.mult, ALU.mult).then_inc(m["yt_full"], 1)
                    if f == 4:
                        for f2 in range(4):
                            low(f2)
                    if f >= 5:
                        low(f - 1)
                low(KT - 1)

            def project_out(layer, z, T):
                n0 = first_unit["out", layer]
                for t in range(KT):
                    if t % 2 == 0:
                        split_lo(dve, n0 + t // 2 + 1)
                    add_squares(z, t, t % 2, T, t == 0)

            split_lo(dve, 0)
            for layer in range(DEPTH):
                m, z = mixer, 3 * layer
                if layer == 0:
                    done = modulation(0, 0, 2, 0, 0)
                else:
                    done = modulation(1, 1, 3, ada_done(("apart", 1)), done)
                norm_in(layer, 0, z, TOK)
                gate_up(layer, 0, 2 * layer, TOK)
                if layer == 0:
                    done = modulation(0, 2, 8, ada_done(("beside", 0, 0)), done)
                else:
                    modulation(1, 3, 9, ada_done(("beside", 1, 0)), done)
                down(layer, 0, z, TOK)
                if layer == 0:
                    done = modulation(0, 8, 9, ada_done("down"), done)
                post_norm(layer, 0, z, TOK, Y_ffn)
                norm_in(layer, 1, z + 1, TOK)
                if layer == 0:
                    done = modulation(1, 0, 1, ada_done(("turn", 0)), done)
                n0 = first_unit["in", layer]
                for u in range(N_PROJ // 2 + 1):
                    split_lo(dve, n0 + u + 1)
                T = width(layer, 1)
                attention(layer, m, T // P)
                gla(layer, m, T)
                mlstm(layer, m, T)
                turn_y(layer, m, T)
                project_out(layer, z + 1, T)
                post_norm(layer, 1, z + 1, T, Y_mix)
                norm_in(layer, 2, z + 2, T)
                gate_up(layer, 1, 2 * layer + 1, T)
                down(layer, 1, z + 2, T)
                post_norm(layer, 2, z + 2, T, Y_ffn)

        @block.tensor
        def _(pe):
            def begin(n, i=0, per=1):
                s, k = n % 2, n // 2 + per * i
                pe.wait_ge(lo_ready[s], k + 1)
                return s

            def ada_tile(j, order, k):
                s = order % 2
                pe.wait_ge(ada_loaded[s], 16 * k + 16)
                for kk in range(KT):
                    last = nc.tensor.matmul(mod_acc[:, bass.ds(j * 2, 2)], ada_slot[s][:, kk, :], silu_c[:, kk:2 * KT:KT],
                                            start=(kk == 0), stop=(kk == KT - 1))
                last.then_inc(ada_used[s], 1)

            def ada_run(name):
                _, j0, count, order = ada_parts[name]

                def body(i):
                    for t in range(2):
                        ada_tile(i * 2 + (j0 + t), order + t, order // 2 + i)
                steps(pe, count // 2, body)

            def first_tile(j):
                g, t = j // 4, j % 4
                pe.wait_ge(first_loaded[g], 16)
                for kk in range(KT):
                    last = nc.tensor.matmul(mod_acc[:, 2 * j:2 * j + 2], ada_first[g][:, kk, t * P:(t + 1) * P],
                                            silu_c[:, kk:2 * KT:KT], start=(kk == 0), stop=(kk == KT - 1))
                last.then_inc(first_used, 1)

            def turn_tiles(z, first, count):
                if ("turn", z) in ada_parts:
                    _, j0, _, order = ada_parts["turn", z]
                    if z == 0:
                        pe.wait_ge(mod_step, 14)
                    for t in range(first, first + count):
                        ada_tile(j0 + t, order + t, (order + t) // 2)

            def norm_in(z, T):
                for k in range(KT):
                    pe.wait_ge(norm["sq_ready"], KT * z + k + 1)
                    nc.tensor.matmul(bank[7][:, 0:T], ones[:], tmp_a[k % 2][:, 0:T], start=(k == 0), stop=(k == KT - 1))\
                        .then_inc(norm["sq_used"], 1)
                    if z == 0 and k % 2 == 0:
                        first_tile(FIRST_TILES - 4 + k // 2)
                    if k % 2 == 1:
                        turn_tiles(z - 1, 2 + k // 2, 1)
                turn_tiles(z - 1, 6, 2)

            def gate_up(layer, q, g, z, T):
                n0 = first_unit[f"gu{q}", layer]
                def body(i):
                    for j in range(2):
                        f = 2 * i + j
                        s = begin(n0 + j, i)
                        wait(pe, gated["prod_ready"], FT * g + f - 1)
                        first = isinstance(i, int) and i + j == 0
                        turns = [(w, k) for k in range(KT) for w in range(2)] if first else \
                            [(w, k) for w in range(2) for k in range(KT)]
                        for w, k in turns:
                            if first and w == 0:
                                pe.wait_ge(norm["u_ready"], KT * z + k + 1)
                            last = products(bank[2 * j + w][:, 0:T], tile_of(w_hi[s], w * DM, k), tile_of(w_lo[s], w * DM, k),
                                            u_hi[:, k, 0:T], u_lo[:, k, 0:T], k == 0, k == KT - 1)
                        last.then_inc(unit_used[s], 1)
                        if ("beside", layer, q) in ada_parts:
                            _, j0, count, order = ada_parts["beside", layer, q]
                            per = count // FT
                            for t in range(per):
                                o = order + j * per + t
                                ada_tile(i * (2 * per) + (j0 + j * per + t), o, o // 2 + i * per)
                steps(pe, FT // 2, body)

            def sum_squares(z, T):
                pe.wait_ge(post["ysq_added"], KT * z + KT)
                nc.tensor.matmul(bank[7][:, 0:T], ones[:], sq_sum[:, 0:T], start=True, stop=True).then_inc(post["ss_done"], 1)
                turn_tiles(z, 0, 2)

            def down(layer, q, g, z, T):
                n0 = first_unit[f"dn{q}", layer]
                pe.wait_ge(gated["ht_ready"], FT * g + FT)
                half = FT // 2

                def body(i):
                    for t in range(2):
                        wait(pe, post["ysq_ready"], KT * z + 2 * i + t - 1)
                        for j in range(2):
                            s = begin(n0 + 2 * t + j, i, 2)
                            for k in range(half):
                                f = j * half + k
                                last = products(bank[4 + t][:, 0:T], tile_of(w_hi[s], 0, k), tile_of(w_lo[s], 0, k),
                                                ht_hi[:, f, 0:T], ht_lo[:, f, 0:T], f == 0, f == FT - 1)
                            last.then_inc(unit_used[s], 1)
                        if (layer, q) == (0, 0):
                            _, j0, _, order = ada_parts["down"]
                            ada_tile(i * 2 + (j0 + t), order + t, order // 2 + i)
                steps(pe, KT // 2, body)
                sum_squares(z, T)

            def project(layer, m, z):
                n0 = first_unit["in", layer]
                for u in range(N_PROJ // 2 + 1):
                    s = begin(n0 + u)
                    wait(pe, m["proj_ready"], 2 * u - 2)
                    for t in range(2 * u, min(2 * u + 2, N_PROJ)):
                        T = width(layer, 1) if t < LAT_ONLY else TOK
                        rows = P if t < T_SMALL else GATE_ROW + 4 * C_HEADS
                        for k in range(KT):
                            if t == 0:
                                pe.wait_ge(norm["u_ready"], KT * z + k + 1)
                            last = products(bank[t % 4][0:rows, 0:T], tile_of(w_hi[s], t % 2 * DM, k)[:, 0:rows],
                                            tile_of(w_lo[s], t % 2 * DM, k)[:, 0:rows],
                                            u_hi[:, k, 0:T], u_lo[:, k, 0:T], k == 0, k == KT - 1)
                    last.then_inc(unit_used[s], 1)

            def project_out(layer, m, z, T):
                n0 = first_unit["out", layer]
                pe.wait_ge(m["yt_ready"], KT)
                for u in range(KT // 2):
                    s = begin(n0 + u)
                    for t in range(2 * u, 2 * u + 2):
                        wait(pe, post["ysq_ready"], KT * z + t - 1)
                        for k in range(KT):
                            last = products(bank[4 + t % 2][:, 0:T], tile_of(w_hi[s], t % 2 * DM, k), tile_of(w_lo[s], t % 2 * DM, k),
                                            u_hi[:, k, 0:T], u_lo[:, k, 0:T], k == 0, k == KT - 1)
                    last.then_inc(unit_used[s], 1)
                sum_squares(z, T)

            def attention(layer, m, NQ):
                pe.wait_ge(m["proj_ready"], N_PROJ)
                for tt in range(TT):
                    for v, t in enumerate(V_TILES):
                        last = nc.tensor.transpose(bank[3 + tt][:, v * P:(v + 1) * P], proj[:, t, tt * P:(tt + 1) * P], ident[:])
                    last.then_inc(m["v_turned"], 1)

                def mlstm_values(g, b):
                    for tt in range(2 * g, 2 * g + 2):
                        for v in range(2):
                            at = (tt % 2 * 2 + v) * P
                            last = nc.tensor.transpose(b[:, at:at + P], proj[:, T_MV + v, tt * P:(tt + 1) * P], ident[:])
                    last.then_inc(m["v_turned"], 1)

                mlstm_values(0, bank[7])
                pe.wait_ge(mix_loaded, 16 * 12 * (layer + 1))
                for b, t, n in ((0, T_Q, 2), (1, T_Q + 2, 2), (2, T_K, 1)):
                    for j in range(n):
                        last = nc.tensor.matmul(bank[b][:, j * LAT:(j + 1) * LAT], rot[:], proj[:, t + j, 0:LAT], start=True, stop=True)
                    last.then_inc(m["rot_done"], 1)
                pe.wait_ge(m["rope_step"], 9)
                nc.tensor.matmul(bank[1][:], swap[:], proj[:, T_K, :], start=True, stop=True).then_inc(m["swap_done"], 1)
                mlstm_values(1, bank[2])
                pe.wait_ge(m["v_ready"], TT)
                pe.wait_ge(m["vm_ready"], 2)
                pe.wait_ge(m["swap_ready"], 1)
                N = A_HEADS * NQ

                def scores(i):
                    qb, h = i // A_HEADS, i % A_HEADS
                    r = h % 2 * A_DIM
                    keys = proj[:, T_K, :] if h // (A_HEADS // A_GROUPS) == h % 2 else k_swapped[:]
                    b = bank[(i % 2) * 2 + i // 2 % 2]
                    wait(pe, m["exp_done"], i - 3)
                    q = proj[r:r + A_DIM, T_Q + h // 2, qb * P:(qb + 1) * P]
                    if qb < 2:
                        nc.tensor.matmul(b[:], q, keys[r:r + A_DIM, :], start=True, stop=False)
                        other = slice((1 - qb) * P, (2 - qb) * P)
                        ins = nc.tensor.matmul(b[:, other], ident[:], band[:, qb, :], start=False, stop=True)
                    else:
                        ins = nc.tensor.matmul(b[:, 0:CTX], q, keys[r:r + A_DIM, LAT:TOK], start=True, stop=True)
                    ins.then_inc(m["score"], 1)

                def turn(i):
                    n = 4 if i // A_HEADS < 2 else 2
                    pe.wait_ge(m["exp_done"], i + 1)
                    wait(pe, m["pt_ready"], i - 1)
                    for cc in range(n):
                        last = nc.tensor.transpose(bank[4 + i % 2][:, cc * P:(cc + 1) * P], probs[i % 3][:, cc * P:(cc + 1) * P], ident[:])
                    last.then_inc(m["turned"], 1)

                def values(i):
                    qb, h = i // A_HEADS, i % A_HEADS
                    first_tile = 0 if qb < 2 else 2
                    n = TT - first_tile
                    g = h // (A_HEADS // A_GROUPS)
                    pe.wait_ge(m["pt_ready"], i + 1)
                    wait(pe, m["o_ready"], i - 1)
                    for cc in range(n):
                        last = nc.tensor.matmul(bank[6 + i % 2][:, 0:A_DIM], probs_t[i % 2][:, cc, :],
                                                v_tok[:, first_tile + cc, g * A_DIM:(g + 1) * A_DIM], start=(cc == 0), stop=(cc == n - 1))
                    last.then_inc(m["pv_done"], 1)

                for i in range(N + 2):
                    if i < N:
                        scores(i)
                    if 1 <= i <= N:
                        turn(i - 1)
                    if i >= 2:
                        values(i - 2)

            def gla(layer, m, T):
                for d in range(2):
                    nc.tensor.matmul(bank[d][:], w_alpha[:, d, :], proj[0:2 * RANK, T_SMALL, :], start=True, stop=True)                        .then_inc(m["gla_z_mm"], 1)
                for lev in range(len(LEVELS) + 1):
                    kq = gla_kq[lev % 2]
                    diagonal = lev == len(LEVELS)
                    if not diagonal:
                        pe.wait_ge(m["gla_k"], lev + 1)
                    pe.wait_ge(m["gla_qs"], lev + 1)
                    for h in range(B_HEADS):
                        r = slice(h * B_DK, (h + 1) * B_DK)
                        if lev in (2, 3):
                            pe.wait_ge(m["gla_put_act"], B_HEADS * (lev - 2) + h + 1)
                        if lev >= 4:
                            pe.wait_ge(m["gla_put"], B_HEADS * (lev - 4) + h + 1)
                        for st in range(T // P):
                            tt = st ^ 1 if lev == 0 else st
                            keys = proj[r, T_GK, st * P:(st + 1) * P] if diagonal else kq[r, 0, st * P:(st + 1) * P]
                            last = nc.tensor.matmul(bank[(lev % 2) * 4 + h][:, st * P:(st + 1) * P], keys,
                                                    kq[r, 1, tt * P:(tt + 1) * P], start=True, stop=True)
                        last.then_inc(m["gla_mm"], 1)
                pe.wait_ge(m["gla_cqk"], 2)
                for h in range(B_HEADS):
                    r = slice(h * B_DK, (h + 1) * B_DK)
                    pe.wait_ge(m["gla_put"], B_HEADS * 5 + h + 1)
                    for st in range(2):
                        for d in range(2):
                            last = nc.tensor.matmul(bank[4 + h][:, st * LAT:(st + 1) * LAT],
                                                    gla_kq[0][r, d, LAT + st * P:LAT + (st + 1) * P], gla_kq[0][r, d, 0:LAT],
                                                    start=(d == 0), stop=(d == 1))
                    last.then_inc(m["gla_cmm"], 1)
                pe.wait_ge(m["gla_put"], B_HEADS * 7)
                pe.wait_ge(m["gla_cput"], B_HEADS)
                for g in range(T // LAT):
                    for tt in range(2 * g, 2 * g + 2):
                        for h in range(B_HEADS):
                            terms = [(gla_diag[:, h, tt, :], tt), (gla_pair[:, h, tt ^ 1, :], tt ^ 1)]
                            if g == 0:
                                terms += [(gla_cross[:, h, j, tt * P:(tt + 1) * P], 2 + j) for j in range(2)]
                            at = tt % 2 * 256 + h * B_DV
                            for e, (sc, st) in enumerate(terms):
                                last = nc.tensor.matmul(bank[g][:, at:at + B_DV], sc, v_tok[:, st, P + h * B_DV:P + (h + 1) * B_DV],
                                                        start=(e == 0), stop=(e == len(terms) - 1))
                    last.then_inc(m["gla_o"], 1)

            def mlstm(layer, m, T):
                NQ = T // P
                for which in range(2):
                    nc.tensor.matmul(bank[6 + which][0:64, :], gate_sel[GATE_ROW:GATE_ROW + 4 * C_HEADS, which, :],
                                     proj[GATE_ROW:GATE_ROW + 4 * C_HEADS, T_SMALL, :], start=True, stop=True).then_inc(m["gate_mm"], 1)
                pe.wait_ge(m["gate_row"], 15)
                for which, rows in enumerate((g_i, g_b)):
                    for tt in range(TT):
                        at = (which * TT + tt) * 64
                        last = nc.tensor.transpose(bank[6][:, at:at + 64], rows[:, tt * P:(tt + 1) * P], ident[0:64, 0:64])
                    last.then_inc(m["gate_turned"], 1)
                pe.wait_ge(m["gate_col"], 2)
                pe.wait_ge(m["qk_ready"], 6)

                def keys_queries(h):
                    r = slice(h % 2 * C_DIM, h % 2 * C_DIM + C_DIM)
                    b0 = 3 * (h % 2)
                    wait(pe, m["p_ready"], 2 * h - 2)
                    blocks = [(0, 0, 0), (1, 2, 0)] + ([(2, 2, LAT)] if T == TOK else [])
                    for b, st0, t0 in blocks:
                        for si in range(2):
                            st = st0 + si
                            last = nc.tensor.matmul(bank[b0 + b][:, si * LAT:(si + 1) * LAT],
                                                    qk_conv[r, 2 + h // 2, st * P:(st + 1) * P],
                                                    qk_conv[r, h // 2, t0:t0 + LAT], start=True, stop=True)
                    last.then_inc(m["kq_done"], 1)

                def numerators(x):
                    h, d = x // 2, x % 2
                    W = w_c[x % 2]
                    pe.wait_ge(m["p_ready"], x + 1)
                    wait(pe, m["hid_step"], 5 * x)
                    for tt in range(NQ):
                        grp, ti = tt // 2, tt % 2
                        cols = slice(ti * P, (ti + 1) * P)
                        terms = [(W[:, grp, si, cols], 2 * grp + si) for si in range(2) if (si <= ti if d == 0 else si >= ti)]
                        if grp == 0:
                            terms += [(W[:, 2, j, cols], 2 + j) for j in range(2)]
                        at = tt * (C_DIM + 1)
                        for e, (wt, st) in enumerate(terms):
                            last = nc.tensor.matmul(bank[7][:, at:at + C_DIM + 1], wt, vm_tok[:, st, h, :],
                                                    start=(e == 0), stop=(e == len(terms) - 1))
                    last.then_inc(m["num_done"], 1)

                for x in range(2 * C_HEADS):
                    h, d = x // 2, x % 2
                    if d == 0:
                        keys_queries(h)
                    wait(pe, m["w_ready"], x)
                    row = 32 * d + h
                    nc.tensor.matmul(bank[6][:], ident[0:64, row:row + 1].to_broadcast([64, P]), g_max[:], start=True, stop=True)                        .then_inc(m["g_done"], 1)
                    if x >= 1:
                        numerators(x - 1)
                numerators(2 * C_HEADS - 1)

            def turn_y(layer, m, T):
                pe.wait_ge(m["y_tok_ready"], 2 * (T // LAT))
                for f in range(KT):
                    for tt in range(T // P):
                        last = nc.tensor.transpose(bank[f][:, tt * P:(tt + 1) * P], y_tok[:, tt, f * P:(f + 1) * P], ident[:])
                    last.then_inc(m["yt_turned"], 1)

            pe.wait_ge(c_loaded, 48)
            pe.wait_ge(c_silu, 1)
            nc.tensor.transpose(bank[0][:, 0:2 * KT], rows_c[:], ident[0:2 * KT, 0:2 * KT]).then_inc(c_turned, 1)
            pe.wait_ge(x_loaded, 32)
            pe.wait_ge(c_ready, 1)
            for k in range(KT):
                wait(pe, x_copied, k - 3)
                for tt in range(TT):
                    last = nc.tensor.transpose(bank[k % 4][:, tt * P:(tt + 1) * P], rows_x[:, tt, k * P:(k + 1) * P], ident[:])
                last.then_inc(x_turned, 1)
            for j in range(FIRST_TILES - 4):
                first_tile(j)
            pe.wait_ge(rows_loaded, 16 * DEPTH * (8 + len(BIAS_RUNS)))
            for la in range(DEPTH):
                for v in range(2):
                    at = (2 * v + la) * P
                    nc.tensor.transpose(bank[4][:, at:at + P], rows_v[2 * la + v][:], ident[:]).then_inc(rows_turned, 1)
            pe.wait_ge(ones_ready, 1)
            for layer in range(DEPTH):
                m, z = mixer, 3 * layer
                if ("apart", layer) in ada_parts:
                    ada_run(("apart", layer))
                norm_in(z, TOK)
                gate_up(layer, 0, 2 * layer, z, TOK)
                down(layer, 0, 2 * layer, z, TOK)
                norm_in(z + 1, TOK)
                project(layer, m, z + 1)
                T = width(layer, 1)
                attention(layer, m, T // P)
                gla(layer, m, T)
                mlstm(layer, m, T)
                turn_y(layer, m, T)
                project_out(layer, m, z + 1, T)
                norm_in(z + 2, T)
                gate_up(layer, 1, 2 * layer + 1, z + 2, T)
                down(layer, 1, 2 * layer + 1, z + 2, T)
            pe.wait_ge(post["h_added"], KT * 3 * DEPTH)
            for t in range(LAT // P):
                for g in range(2):
                    for cc in range(4):
                        last = nc.tensor.transpose(bank[2 * t + g][:, cc * P:(cc + 1) * P], H[:, 4 * g + cc, t * P:(t + 1) * P], ident[:])
                    last.then_inc(out_turned, 1)


_INS = ['x', 'c', 'ctx', 'c_ctx', 'ada_w', 'ada_b', 'norm_g', 'ffn1_wg', 'ffn1_wu', 'ffn1_wd', 'ffn2_wg', 'ffn2_wu',
        'ffn2_wd', 'w_in', 'b_in', 'w_out', 'attn_sink', 'gla_w_alpha', 'gla_b_alpha', 'gla_norm', 'mlstm_conv',
        'mlstm_f_bias', 'mlstm_norm']
_OUTS = [((1, LAT, DM), 'float32')]


def _constants():
    import numpy as np
    ident = np.eye(P, dtype=np.float32)
    rot = np.zeros((P, P), np.float32)
    swap = np.zeros((P, P), np.float32)
    for i in range(P):
        if i % 32 < 16:
            rot[i + 16, i] = -1.0
        else:
            rot[i - 16, i] = 1.0
        swap[(i + 64) % P, i] = 1.0
    half = 16
    inv_freq = np.float32(10000.0) ** (-np.arange(half, dtype=np.float32) / np.float32(half))
    tok = np.arange(LAT)
    rows, cols = (tok // 64).astype(np.float32), (tok % 64).astype(np.float32)
    angle = np.zeros((P, LAT), np.float32)
    for p in range(P):
        angle[p] = (rows if p % 64 < 32 else cols) * inv_freq[p % 16]
    i, j = np.arange(P)[:, None], np.arange(P)[None, :]
    band = np.stack([np.where(j <= i, 0.0, NEG), np.where(j >= i, 0.0, NEG)]).astype(np.float32)
    level = [((i // (2 * h) == j // (2 * h)) & (i // h != j // h)) for h in MASKED] + [i == j]
    sel = np.zeros((4 * C_HEADS, 2, 64), np.float32)
    for d in range(2):
        for h in range(C_HEADS):
            sel[8 * d + 4 + h, 0, 32 * d + h] = 1.0
            sel[8 * d + h, 1, 32 * d + h] = 1.0
    return {"k_ident": ident, "k_rot": rot, "k_swap": swap, "k_cos": np.cos(angle), "k_sin": np.sin(angle),
            "k_band": band, "k_level": np.stack(level).astype(np.float32), "k_sel": sel}


def kernel(**inputs):
    import numpy as _np
    import concourse.bacc as _bacc
    from concourse import mybir as _mybir
    from concourse.bass_utils import run_bass_kernel_spmd as _run

    nc = _bacc.Bacc("TRN2", target_bir_lowering=False, num_devices=1)
    arrays, args = {}, []
    for name in _INS:
        arrays[f"in_{name}_dram"] = _np.ascontiguousarray(inputs[name])
    for name, a in _constants().items():
        arrays[f"in_{name}_dram"] = a
    for name, a in arrays.items():
        args.append(nc.dram_tensor(name, a.shape, _mybir.dt.from_np(a.dtype), kind="ExternalInput").ap())
    for i, (shape, dtype) in enumerate(_OUTS):
        dt = _mybir.dt.from_np(_np.dtype(dtype))
        args.append(nc.dram_tensor(f"out_{i}_dram", shape, dt, kind="ExternalOutput").ap())
    hybrid_block_kernel(nc, *args)
    r = _run(nc, [arrays], core_ids=[0])
    got = tuple(r.results[0][f"out_{i}_dram"] for i in range(len(_OUTS)))
    return got[0]
```
